# Optimizing a Trainium2 kernel written in Bass

```python
import math
import jax, jax.numpy as jnp
from jax import lax
import numpy as np

D_MODEL = 2048
BATCH = 1
SEQ = 256
DEPTH = 1

N_HEADS = 8
HEAD_DIM = 128
ATTN_W = N_HEADS * HEAD_DIM
MOBA_BLOCK = 256
MOBA_TOPK = 3
MOBA_QCHUNK = 64
N_BUCKETS = 32
MAX_DISTANCE = 128
LRU_W = D_MODEL // 2
LRU_BLOCKS = 8
LRU_BW = LRU_W // LRU_BLOCKS
LRU_CONV = 4
LRU_C = 8.0
SC_W = D_MODEL // 2
SC_CONV = 3
D_FF = 4 * D_MODEL
N_BRANCH = 3
EPS = 1e-6
IN_SPLITS = (ATTN_W, ATTN_W, ATTN_W, LRU_W, LRU_W, SC_W, SC_W, SC_W, N_BRANCH * D_MODEL)
N_IN = sum(IN_SPLITS)


def rms_norm(x, g):
    xf = x.astype(jnp.float32)
    y = xf * lax.rsqrt(jnp.mean(xf * xf, axis=-1, keepdims=True) + EPS)
    return (y * g.astype(jnp.float32)).astype(x.dtype)

def causal_depthwise_conv(x, w):
    k = w.shape[0]
    return lax.conv_general_dilated(
        x, w[:, None, :].astype(x.dtype), window_strides=(1,), padding=[(k - 1, 0)],
        dimension_numbers=('NWC', 'WIO', 'NWC'), feature_group_count=x.shape[-1])

def t5_bucket(dist):
    n = jnp.maximum(dist, 0)
    max_exact = N_BUCKETS // 2
    nf = jnp.maximum(n, 1).astype(jnp.float32)
    large = max_exact + (jnp.log(nf / max_exact) / math.log(MAX_DISTANCE / max_exact)
                         * (N_BUCKETS - max_exact)).astype(jnp.int32)
    large = jnp.minimum(large, N_BUCKETS - 1)
    return jnp.where(n < max_exact, n, large)

def moba_attention(q, k, v, rel_table):
    bsz, seq, n_heads, d_head = q.shape
    n_blk = -(-seq // MOBA_BLOCK)
    s_pad = n_blk * MOBA_BLOCK
    topk = min(MOBA_TOPK, n_blk)
    pad = ((0, 0), (0, s_pad - seq), (0, 0), (0, 0))
    qh = jnp.pad(q * (d_head ** -0.5), pad).transpose(0, 2, 1, 3)
    kh = jnp.pad(k, pad).transpose(0, 2, 1, 3)
    vh = jnp.pad(v, pad).transpose(0, 2, 1, 3)
    kb = kh.reshape(bsz, n_heads, n_blk, MOBA_BLOCK, d_head)
    vb = vh.reshape(bsz, n_heads, n_blk, MOBA_BLOCK, d_head)
    k_mean = jnp.mean(kb.astype(jnp.float32), axis=3)
    gate = jnp.einsum('bhsd,bhnd->bhsn', qh.astype(jnp.float32), k_mean)
    q_blk = jnp.arange(s_pad) // MOBA_BLOCK
    past = jnp.arange(n_blk)[None, :] < q_blk[:, None]
    gate = jnp.where(past, gate, -jnp.inf)
    _, sel = lax.top_k(gate, topk)
    slot_ok = jnp.arange(topk)[None, :] < q_blk[:, None]
    b_idx = jnp.arange(bsz)[:, None, None, None]
    h_idx = jnp.arange(n_heads)[None, :, None, None]
    tbl_hb = rel_table.T
    blk_pos = jnp.arange(MOBA_BLOCK)

    def chunk(c):
        start = c * MOBA_QCHUNK
        qc = lax.dynamic_slice_in_dim(qh, start, MOBA_QCHUNK, axis=2)
        sel_c = lax.dynamic_slice_in_dim(sel, start, MOBA_QCHUNK, axis=2)
        ok_c = lax.dynamic_slice_in_dim(slot_ok, start, MOBA_QCHUNK, axis=0)
        q_pos = start + jnp.arange(MOBA_QCHUNK)
        kg = kb[b_idx, h_idx, sel_c]
        vg = vb[b_idx, h_idx, sel_c]
        s_past = jnp.einsum('bhqd,bhqnkd->bhqnk', qc, kg, preferred_element_type=jnp.float32)
        k_pos = sel_c[..., None] * MOBA_BLOCK + blk_pos
        bkt = t5_bucket(q_pos[:, None, None] - k_pos)
        s_past = s_past + tbl_hb[h_idx[..., None], bkt]
        s_past = jnp.where(ok_c[:, :, None], s_past, -jnp.inf)
        own = start // MOBA_BLOCK
        k_own = lax.dynamic_index_in_dim(kb, own, axis=2, keepdims=False)
        v_own = lax.dynamic_index_in_dim(vb, own, axis=2, keepdims=False)
        s_own = jnp.einsum('bhqd,bhkd->bhqk', qc, k_own, preferred_element_type=jnp.float32)
        dist = q_pos[:, None] - (own * MOBA_BLOCK + blk_pos)[None, :]
        s_own = s_own + rel_table[t5_bucket(dist)].transpose(2, 0, 1)
        s_own = jnp.where(dist >= 0, s_own, -jnp.inf)
        logits = jnp.concatenate(
            [s_past.reshape(bsz, n_heads, MOBA_QCHUNK, topk * MOBA_BLOCK), s_own], axis=-1)
        p = jax.nn.softmax(logits, axis=-1)
        p_past = p[..., :topk * MOBA_BLOCK].reshape(bsz, n_heads, MOBA_QCHUNK, topk, MOBA_BLOCK)
        p_own = p[..., topk * MOBA_BLOCK:]
        o = (jnp.einsum('bhqnk,bhqnkd->bhqd', p_past.astype(vg.dtype), vg,
                        preferred_element_type=jnp.float32)
             + jnp.einsum('bhqk,bhkd->bhqd', p_own.astype(v_own.dtype), v_own,
                          preferred_element_type=jnp.float32))
        return o.astype(q.dtype)

    out = lax.map(chunk, jnp.arange(s_pad // MOBA_QCHUNK))
    out = out.transpose(1, 0, 3, 2, 4).reshape(bsz, s_pad, n_heads * d_head)
    return out[:, :seq]

def _lru_combine(c1, c2):
    a1, b1 = c1
    a2, b2 = c2
    return a1 * a2, a2 * b1 + b2

def rg_lru_branch(xr, gate_br, conv_w, conv_b, wa, ba, wx, bx, lam):
    xc = causal_depthwise_conv(xr, conv_w) + conv_b
    bsz, seq, width = xc.shape
    xg = xc.reshape(bsz, seq, LRU_BLOCKS, LRU_BW)
    r = jax.nn.sigmoid((jnp.einsum('bsgi,gij->bsgj', xg, wa).reshape(bsz, seq, width) + ba)
                       .astype(jnp.float32))
    i = jax.nn.sigmoid((jnp.einsum('bsgi,gij->bsgj', xg, wx).reshape(bsz, seq, width) + bx)
                       .astype(jnp.float32))
    log_a = -LRU_C * r * jax.nn.softplus(-lam.astype(jnp.float32))
    a = jnp.exp(log_a)
    mult = jnp.sqrt(-jnp.expm1(2.0 * log_a))
    u = mult * i * xc.astype(jnp.float32)
    _, h = lax.associative_scan(_lru_combine, (a, u), axis=1)
    return (h * jax.nn.gelu(gate_br.astype(jnp.float32))).astype(xr.dtype)

def short_conv_branch(b, c, xs, conv_w):
    return b * causal_depthwise_conv(c * xs, conv_w)

def first_inputs(seed: int = 0) -> dict:
    key = jax.random.key(seed)
    ks = jax.random.split(key, 24)
    f32 = jnp.float32
    nrm = lambda k, shape, fan_in: jax.random.normal(k, shape, f32) * (fan_in ** -0.5)
    u = jax.random.uniform(ks[12], (DEPTH, LRU_W), f32, minval=0.9, maxval=0.999)
    a_base = u ** (1.0 / LRU_C)
    lam = jnp.log(a_base) - jnp.log1p(-a_base)
    return {
        "x": jax.random.normal(ks[0], (BATCH, SEQ, D_MODEL), f32),
        "norm_mix_g": 1.0 + 0.02 * jax.random.normal(ks[1], (DEPTH, D_MODEL), f32),
        "w_in": nrm(ks[2], (DEPTH, D_MODEL, N_IN), D_MODEL),
        "gate_b": 0.02 * jax.random.normal(ks[3], (DEPTH, N_BRANCH * D_MODEL), f32),
        "rel_table": 0.1 * jax.random.normal(ks[4], (N_BUCKETS, N_HEADS), f32),
        "w_attn_o": nrm(ks[5], (DEPTH, ATTN_W, D_MODEL), ATTN_W),
        "lru_conv_w": nrm(ks[6], (DEPTH, LRU_CONV, LRU_W), LRU_CONV),
        "lru_conv_b": 0.02 * jax.random.normal(ks[7], (DEPTH, LRU_W), f32),
        "lru_wa": nrm(ks[8], (DEPTH, LRU_BLOCKS, LRU_BW, LRU_BW), LRU_BW),
        "lru_ba": 0.02 * jax.random.normal(ks[9], (DEPTH, LRU_W), f32),
        "lru_wx": nrm(ks[10], (DEPTH, LRU_BLOCKS, LRU_BW, LRU_BW), LRU_BW),
        "lru_bx": 0.02 * jax.random.normal(ks[11], (DEPTH, LRU_W), f32),
        "lru_lambda": lam,
        "w_lru_o": nrm(ks[13], (DEPTH, LRU_W, D_MODEL), LRU_W),
        "sc_conv_w": nrm(ks[14], (DEPTH, SC_CONV, SC_W), SC_CONV),
        "w_sc_o": nrm(ks[15], (DEPTH, SC_W, D_MODEL), SC_W),
        "w_out": nrm(ks[16], (DEPTH, D_MODEL, D_MODEL), D_MODEL),
        "norm_mlp_g": 1.0 + 0.02 * jax.random.normal(ks[17], (DEPTH, D_MODEL), f32),
        "w_mlp_up": nrm(ks[18], (DEPTH, D_MODEL, D_FF), D_MODEL),
        "w_mlp_down": nrm(ks[19], (DEPTH, D_FF, D_MODEL), D_FF),
        "final_g": 1.0 + 0.02 * jax.random.normal(ks[20], (D_MODEL,), f32),
    }

def first_block(x, norm_mix_g, w_in, gate_b, rel_table, w_attn_o, lru_conv_w, lru_conv_b,
              lru_wa, lru_ba, lru_wx, lru_bx, lru_lambda, w_lru_o, sc_conv_w, w_sc_o,
              w_out, norm_mlp_g, w_mlp_up, w_mlp_down, final_g):
    bsz, seq, _ = x.shape
    offs = np.cumsum(IN_SPLITS)[:-1].tolist()
    for l in range(DEPTH):
        h = rms_norm(x, norm_mix_g[l])
        proj = h @ w_in[l]
        q, k, v, xr, gr, sc_b, sc_c, sc_x, g_pre = jnp.split(proj, offs, axis=-1)
        heads = (bsz, seq, N_HEADS, HEAD_DIM)
        y_a = moba_attention(q.reshape(heads), k.reshape(heads), v.reshape(heads),
                             rel_table) @ w_attn_o[l]
        y_b = rg_lru_branch(xr, gr, lru_conv_w[l], lru_conv_b[l], lru_wa[l], lru_ba[l],
                            lru_wx[l], lru_bx[l], lru_lambda[l]) @ w_lru_o[l]
        y_c = short_conv_branch(sc_b, sc_c, sc_x, sc_conv_w[l]) @ w_sc_o[l]
        g_a, g_b, g_c = jnp.split(jax.nn.sigmoid(g_pre + gate_b[l]), N_BRANCH, axis=-1)
        x = x + (g_a * y_a + g_b * y_b + g_c * y_c) @ w_out[l]
        h = rms_norm(x, norm_mlp_g[l])
        x = x + jnp.square(jax.nn.relu(h @ w_mlp_up[l])) @ w_mlp_down[l]
    return rms_norm(x, final_g)


SSD_WIDTH = D_MODEL // 2
SSD_HEAD_DIM = 64
SSD_HEADS = SSD_WIDTH // SSD_HEAD_DIM
SSD_GROUPS = 2
SSD_STATE = 128
SSD_CONV = 4
SSD_CHUNK = 128
ATT_WIDTH = D_MODEL - SSD_WIDTH
ATT_HEAD_DIM = 128
ATT_HEADS = ATT_WIDTH // ATT_HEAD_DIM
ATT_KV_HEADS = 4
IDX_HEADS = 16
IDX_HEAD_DIM = 64
IDX_TOPK_MAX = 256
Q_BLOCK = 128
D_FF_2 = 4 * D_MODEL
MIX_WIDTH = SSD_WIDTH + ATT_WIDTH
DT_COL_SCALE = 0.1

N_Z = SSD_WIDTH
N_BC = SSD_GROUPS * SSD_STATE
CONV_CH = SSD_WIDTH + 2 * N_BC
N_DT = SSD_HEADS
N_Q = ATT_HEADS * ATT_HEAD_DIM
N_KV = ATT_KV_HEADS * ATT_HEAD_DIM
N_QI = IDX_HEADS * IDX_HEAD_DIM
N_KI = IDX_HEAD_DIM
N_WI = IDX_HEADS
IN_SIZES = (N_Z, CONV_CH, N_DT, N_Q, N_KV, N_KV, N_QI, N_KI, N_WI)
IN_WIDTH = N_Z + CONV_CH + N_DT + N_Q + 2 * N_KV + N_QI + N_KI + N_WI


def _split(t, sizes):
    pts = [int(v) for v in np.cumsum(sizes)[:-1]]
    return jnp.split(t, pts, axis=-1)

def rmsnorm(x, g):
    xf = x.astype(jnp.float32)
    y = xf * lax.rsqrt(jnp.mean(xf * xf, axis=-1, keepdims=True) + EPS)
    return (y * g.astype(jnp.float32)).astype(x.dtype)

def causal_dwconv(u, w, bias):
    ch = u.shape[-1]
    out = lax.conv_general_dilated(
        u, w[:, None, :], window_strides=(1,), padding=((SSD_CONV - 1, 0),),
        dimension_numbers=("NWC", "WIO", "NWC"), feature_group_count=ch)
    return out + bias

def ssd_chunked(xs, dt, a, bm, cm):
    b, l, h, p = xs.shape
    g, n = bm.shape[-2:]
    r = h // g
    q = SSD_CHUNK
    c = l // q
    xdt = (xs * dt[..., None]).reshape(b, c, q, g, r, p)
    adt = (dt * a).reshape(b, c, q, g, r)
    bm = bm.reshape(b, c, q, g, n)
    cm = cm.reshape(b, c, q, g, n)
    a_cum = jnp.cumsum(adt, axis=2)
    seg = a_cum[:, :, :, None] - a_cum[:, :, None, :]
    causal = jnp.tril(jnp.ones((q, q), dtype=bool))[None, None, :, :, None, None]
    decay = jnp.exp(jnp.where(causal, seg, -jnp.inf))
    cb = jnp.einsum("bclgn,bcsgn->bclsg", cm, bm)
    y_diag = jnp.einsum("bclsg,bclsgr,bcsgrp->bclgrp", cb, decay, xdt)
    decay_state = jnp.exp(a_cum[:, :, -1:] - a_cum)
    states = jnp.einsum("bcsgn,bcsgr,bcsgrp->bcgrpn", bm, decay_state, xdt)
    chunk_decay = jnp.exp(a_cum[:, :, -1])

    def step(carry, inp):
        st, dec = inp
        return carry * dec[..., None, None] + st, carry

    init = jnp.zeros((b, g, r, p, n), dtype=xs.dtype)
    _, prev = lax.scan(step, init, (jnp.swapaxes(states, 0, 1), jnp.swapaxes(chunk_decay, 0, 1)))
    prev = jnp.swapaxes(prev, 0, 1)
    y_off = jnp.einsum("bclgn,bcgrpn,bclgr->bclgrp", cm, prev, jnp.exp(a_cum))
    return (y_diag + y_off).reshape(b, l, h, p)

def dsa_attention(q, k, v, q_idx, k_idx, w_idx):
    b, l = q.shape[:2]
    topk = min(IDX_TOPK_MAX, l // 4)
    qb = min(Q_BLOCK, l)
    nb = l // qb
    rep = ATT_HEADS // ATT_KV_HEADS
    key_pos = jnp.arange(l)

    def to_blocks(t):
        return jnp.swapaxes(t.reshape(b, nb, qb, *t.shape[2:]), 0, 1)

    def one_block(args):
        q_b, qi_b, wi_b, start = args
        t_pos = start + jnp.arange(qb)
        s = jnp.einsum("bqhd,bsd->bqhs", qi_b, k_idx) * (IDX_HEAD_DIM ** -0.5)
        score = jnp.einsum("bqhs,bqh->bqs", jax.nn.relu(s), wi_b).astype(jnp.float32)
        admissible = key_pos[None, :] <= t_pos[:, None]
        score = jnp.where(admissible[None], score, -jnp.inf)
        _, sel = lax.top_k(score, topk)
        sel_ok = sel <= t_pos[None, :, None]
        k_sel = jax.vmap(lambda kk, ii: kk[ii])(k, sel)
        v_sel = jax.vmap(lambda vv, ii: vv[ii])(v, sel)
        qg = q_b.reshape(b, qb, ATT_KV_HEADS, rep, ATT_HEAD_DIM)
        logits = jnp.einsum("bqhgd,bqkhd->bqhgk", qg, k_sel).astype(jnp.float32) * (ATT_HEAD_DIM ** -0.5)
        logits = jnp.where(sel_ok[:, :, None, None, :], logits, -jnp.inf)
        prob = jax.nn.softmax(logits, axis=-1).astype(v.dtype)
        o = jnp.einsum("bqhgk,bqkhd->bqhgd", prob, v_sel)
        return o.reshape(b, qb, ATT_HEADS * ATT_HEAD_DIM)

    starts = jnp.arange(nb, dtype=jnp.int32) * qb
    out = lax.map(one_block, (to_blocks(q), to_blocks(q_idx), to_blocks(w_idx), starts))
    return jnp.swapaxes(out, 0, 1).reshape(b, l, ATT_HEADS * ATT_HEAD_DIM)

def hybrid_layer(x, g_mix, w_in, conv_w, conv_b, dt_bias, a_log, d_skip, g_ssd,
                 g_q, g_k, g_kidx, w_out, g_mlp, w_up, w_down):
    b, l, _ = x.shape
    h = rmsnorm(x, g_mix) @ w_in
    z, xbc, dt, q, k, v, qi, ki, wi = _split(h, IN_SIZES)

    xbc = jax.nn.silu(causal_dwconv(xbc, conv_w, conv_b))
    xs, bm, cm = _split(xbc, (SSD_WIDTH, N_BC, N_BC))
    xs_f = xs.astype(jnp.float32).reshape(b, l, SSD_HEADS, SSD_HEAD_DIM)
    dt_f = jax.nn.softplus(dt.astype(jnp.float32) + dt_bias.astype(jnp.float32))
    a = -jnp.exp(a_log.astype(jnp.float32))
    y = ssd_chunked(xs_f, dt_f, a,
                    bm.astype(jnp.float32).reshape(b, l, SSD_GROUPS, SSD_STATE),
                    cm.astype(jnp.float32).reshape(b, l, SSD_GROUPS, SSD_STATE))
    y = y + d_skip.astype(jnp.float32)[:, None] * xs_f
    y = y.reshape(b, l, SSD_WIDTH) * jax.nn.silu(z.astype(jnp.float32))
    yg = y.reshape(b, l, SSD_GROUPS, SSD_WIDTH // SSD_GROUPS)
    yg = yg * lax.rsqrt(jnp.mean(yg * yg, axis=-1, keepdims=True) + EPS)
    y_ssd = (yg.reshape(b, l, SSD_WIDTH) * g_ssd.astype(jnp.float32)).astype(x.dtype)

    q = rmsnorm(q.reshape(b, l, ATT_HEADS, ATT_HEAD_DIM), g_q)
    k = rmsnorm(k.reshape(b, l, ATT_KV_HEADS, ATT_HEAD_DIM), g_k)
    v = v.reshape(b, l, ATT_KV_HEADS, ATT_HEAD_DIM)
    qi = qi.reshape(b, l, IDX_HEADS, IDX_HEAD_DIM)
    ki = rmsnorm(ki, g_kidx)
    wi = wi * (IDX_HEADS ** -0.5)
    y_att = dsa_attention(q, k, v, qi, ki, wi)

    x = x + jnp.concatenate([y_ssd, y_att], axis=-1) @ w_out

    u = rmsnorm(x, g_mlp) @ w_up
    return x + jnp.square(jax.nn.relu(u)) @ w_down

def second_inputs(seed: int = 0) -> dict:
    key = jax.random.key(seed)
    ks = jax.random.split(key, 20)
    f32 = jnp.float32
    nrm = lambda k, shape, s: jax.random.normal(k, shape, f32) * s
    gain = lambda k, shape: 1.0 + 0.02 * jax.random.normal(k, shape, f32)

    x = jax.random.normal(ks[0], (BATCH, SEQ, D_MODEL), f32)
    col_scale = jnp.ones((IN_WIDTH,), f32).at[N_Z + CONV_CH:N_Z + CONV_CH + N_DT].set(DT_COL_SCALE)
    w_in = nrm(ks[1], (DEPTH, D_MODEL, IN_WIDTH), D_MODEL ** -0.5) * col_scale
    conv_w = nrm(ks[2], (DEPTH, SSD_CONV, CONV_CH), SSD_CONV ** -0.5)
    conv_b = nrm(ks[3], (DEPTH, CONV_CH), 0.01)
    u = jax.random.uniform(ks[4], (DEPTH, SSD_HEADS), f32)
    dt0 = jnp.exp(u * (jnp.log(0.1) - jnp.log(0.001)) + jnp.log(0.001))
    dt_bias = dt0 + jnp.log(-jnp.expm1(-dt0))
    a_log = jnp.log(jax.random.uniform(ks[5], (DEPTH, SSD_HEADS), f32, 1.0, 16.0))
    d_skip = 1.0 + 0.1 * jax.random.normal(ks[6], (DEPTH, SSD_HEADS), f32)
    return {
        "x": x,
        "g_mix": gain(ks[7], (DEPTH, D_MODEL)),
        "w_in": w_in,
        "conv_w": conv_w,
        "conv_b": conv_b,
        "dt_bias": dt_bias,
        "a_log": a_log,
        "d_skip": d_skip,
        "g_ssd": gain(ks[8], (DEPTH, SSD_WIDTH)),
        "g_q": gain(ks[9], (DEPTH, ATT_HEAD_DIM)),
        "g_k": gain(ks[10], (DEPTH, ATT_HEAD_DIM)),
        "g_kidx": gain(ks[11], (DEPTH, IDX_HEAD_DIM)),
        "w_out": nrm(ks[12], (DEPTH, MIX_WIDTH, D_MODEL), MIX_WIDTH ** -0.5),
        "g_mlp": gain(ks[13], (DEPTH, D_MODEL)),
        "w_up": nrm(ks[14], (DEPTH, D_MODEL, D_FF_2), D_MODEL ** -0.5),
        "w_down": nrm(ks[15], (DEPTH, D_FF_2, D_MODEL), D_FF_2 ** -0.5),
    }

def second_block(x, g_mix, w_in, conv_w, conv_b, dt_bias, a_log, d_skip, g_ssd,
              g_q, g_k, g_kidx, w_out, g_mlp, w_up, w_down):
    for i in range(DEPTH):
        x = hybrid_layer(x, g_mix[i], w_in[i], conv_w[i], conv_b[i], dt_bias[i], a_log[i],
                         d_skip[i], g_ssd[i], g_q[i], g_k[i], g_kidx[i], w_out[i],
                         g_mlp[i], w_up[i], w_down[i])
    return x


def setup_inputs(seed=0):
    out = dict(first_inputs(seed))
    for name, value in second_inputs(seed + 1).items():
        if name != "x":
            out[name + "_2"] = value
    return out


def reference(
    x, norm_mix_g, w_in, gate_b, rel_table, w_attn_o, lru_conv_w, lru_conv_b, lru_wa, lru_ba,
    lru_wx, lru_bx, lru_lambda, w_lru_o, sc_conv_w, w_sc_o, w_out, norm_mlp_g, w_mlp_up,
    w_mlp_down, final_g, g_mix_2, w_in_2, conv_w_2, conv_b_2, dt_bias_2, a_log_2, d_skip_2,
    g_ssd_2, g_q_2, g_k_2, g_kidx_2, w_out_2, g_mlp_2, w_up_2, w_down_2,
):
    x = first_block(
        x, norm_mix_g, w_in, gate_b, rel_table, w_attn_o, lru_conv_w, lru_conv_b, lru_wa,
        lru_ba, lru_wx, lru_bx, lru_lambda, w_lru_o, sc_conv_w, w_sc_o, w_out, norm_mlp_g,
        w_mlp_up, w_mlp_down, final_g,
    )
    return second_block(
        x, g_mix_2, w_in_2, conv_w_2, conv_b_2, dt_bias_2, a_log_2, d_skip_2, g_ssd_2, g_q_2,
        g_k_2, g_kidx_2, w_out_2, g_mlp_2, w_up_2, w_down_2,
    )


_drawn_inputs = setup_inputs


def setup_inputs(seed=0):
    import zlib

    import numpy as np

    out = dict(_drawn_inputs(seed))
    spreads = {}
    factors = {'gate_b': 6.342,
     'rel_table': 3.851,
     'lru_ba': 8.0,
     'lru_bx': 8.0,
     'conv_b_2': 6.881,
     'g_ssd_2': 4.582,
     'g_q_2': 8.0,
     'g_k_2': 8.0,
     'g_kidx_2': 5.306,
     'g_mlp_2': 3.439}
    for name, (base, spread) in spreads.items():
        noise = np.random.default_rng([zlib.crc32(name.encode()), seed]).standard_normal(out[name].shape)
        drawn = base * np.exp(spread * noise) if base else spread * noise
        out[name] = __import__('jax').numpy.asarray(drawn.astype(out[name].dtype))
    for name, factor in factors.items():
        out[name] = (out[name] * factor).astype(out[name].dtype)
    return out
```

```python
from contextlib import ExitStack

import numpy as np

import concourse.bass as bass
from concourse import mybir

F32 = mybir.dt.float32
F32R = mybir.dt.float32r
ALU = mybir.AluOpType
ACT = mybir.ActivationFunctionType
AX_X = mybir.AxisListType.X
ds = bass.ds

P = 128
T = 256
D = 2048
DT = D // P
KC = 8
CW = KC * P
NSLOT = 4
LEAD = 4
HEADS = 8
FF_GROUPS = 4
EPS = 1e-6
NEG = -1e30
TAKEN = -3e38
QK_SCALE = float(P) ** -0.5
GELU_C0 = 0.7978845608028654
GELU_C1 = GELU_C0 * 0.044715

L1_CHUNKS = 8 * 16
Y_CHUNKS = 16 * 9
OUT_CHUNKS = 32
MLP_CHUNKS = FF_GROUPS * 64
L2_UNITS = 1 + 4 + 4 + 8 + 12 + 16
B_Y = L1_CHUNKS
B_OUT1 = B_Y + Y_CHUNKS
B_MLP1 = B_OUT1 + OUT_CHUNKS
B_L2 = B_MLP1 + MLP_CHUNKS
B_OUT2 = B_L2 + 2 * L2_UNITS
B_MLP2 = B_OUT2 + OUT_CHUNKS
CHUNKS = B_MLP2 + MLP_CHUNKS

A_Y = 64
A_OUT1 = A_Y + 96
A_MLP1 = A_OUT1 + 16
A_L2 = A_MLP1 + FF_GROUPS * 32
A_OUT2 = A_L2 + L2_UNITS
A_MLP2 = A_OUT2 + 16

PARAMS = {}
_at = 0
for _name, _n in [
    ("g_mix1", 16), ("gate_b", 48), ("lru_w", 32), ("lru_b", 8), ("lru_ba", 8), ("lru_bx", 8), ("lam", 8),
    ("sc_w", 24), ("g_mlp1", 16), ("final_g", 16), ("g_mix2", 16), ("conv_w", 48), ("conv_b", 12),
    ("g_mlp2", 16), ("g_ssd", 8), ("d_skip", 8), ("g_q", 1), ("g_k", 1), ("g_kidx", 1), ("dt_bias", 1),
    ("a_log", 1),
]:
    PARAMS[_name] = _at
    _at += _n
N_PARAMS = _at
DT_ROW = 96
WI_COL = 64


class At:

    def __init__(self, base, *terms):
        self.base, self.terms = base, terms

    def plus(self, k):
        return At(self.base + k, *self.terms)

    def times(self, k):
        return At(self.base * k, *[(i, s * k) for i, s in self.terms])

    def value(self, k=0):
        v = self.base + k
        for i, step in self.terms:
            v = i * step + v
        return v

    def mod(self, n):
        assert all(s % n == 0 for _, s in self.terms)
        return self.base % n

    def div(self, n):
        assert all(s % n == 0 for _, s in self.terms)
        return At(self.base // n, *[(i, s // n) for i, s in self.terms])

    def least(self):
        return self.base


class Steps:

    def __init__(self, eng, sem, per, rnd):
        self.eng, self.sem, self.per, self.rnd, self.k = eng, sem, per, rnd, 0

    def step(self, ins):
        ins.then_inc(self.sem, 1)
        self.k += 1
        assert self.k <= self.per

    def wait(self, k=None, eng=None):
        (eng or self.eng).wait_ge(self.sem, self.rnd.times(self.per).value(self.k if k is None else k))


class Semaphores:

    def __init__(self, make):
        self.ssd_sum = make("ssd_sum")
        self.staged = make("staged")
        self.xs_staged = make("xs_staged")
        self.x_landed = make("x_landed")
        self.x_landed2 = make("x_landed2")
        self.par_landed = make("par_landed")
        self.cst_landed = make("cst_landed")
        self.oh_landed = make("oh_landed")
        self.tab_landed = make("tab_landed")
        self.pads = make("pads")
        self.hi_done = make("hi_done")
        self.lo_done = make("lo_done")
        self.mm_done = make("mm_done")
        self.evacuated = make("evacuated")
        self.a_hi_ready = make("a_hi_ready")
        self.a_ready = make("a_ready")
        self.sq_ready = make("sq_ready")
        self.sq_added = make("sq_added")
        self.sq_zeroed = make("sq_zeroed")
        self.stat_ready = make("stat_ready")
        self.var_ready = make("var_ready")
        self.std_ready = make("std_ready")
        self.r_steps = make("r_steps")
        self.x2_dve = make("x2_dve")
        self.setup_act = make("setup_act")
        self.setup_dve = make("setup_dve")
        self.sp_dve = make("sp_dve")
        self.sp_act = make("sp_act")
        self.bias_ps = make("bias_ps")
        self.bias_copied = make("bias_copied")
        self.causal_landed = make("causal_landed")
        self.bias_in = make("bias_in")
        self.scores_ready = make("scores_ready")
        self.logits_ready = make("logits_ready")
        self.nmax_ready = make("nmax_ready")
        self.probs_exp = make("probs_exp")
        self.den_inv = make("den_inv")
        self.probs_ready = make("probs_ready")
        self.probs_transposed = make("probs_transposed")
        self.pt_copied = make("pt_copied")
        self.v_transposed = make("v_transposed")
        self.v_copied = make("v_copied")
        self.pv_done = make("pv_done")
        self.attn_hi = make("attn_hi")
        self.attn_ready = make("attn_ready")
        self.lru_dve = make("lru_dve")
        self.lru_act = make("lru_act")
        self.lru_pe = make("lru_pe")
        self.sc_dve = make("sc_dve")
        self.sc_act = make("sc_act")
        self.gate_th = make("gate_th")
        self.mix_dve = make("mix_dve")
        self.mix_hi = make("mix_hi")
        self.mix_ready = make("mix_ready")
        self.up_dve = make("up_dve")
        self.hid_hi = make("hid_hi")
        self.hid_ready = make("hid_ready")
        self.fin_act = make("fin_act")
        self.sm_pe = make("sm_pe")
        self.sm_act = make("sm_act")
        self.sm_dve = make("sm_dve")
        self.sm_dma = make("sm_dma")
        self.cleared = make("cleared")
        self.nh_sq = make("nh_sq")
        self.nh_ready = make("nh_ready")
        self.vt_pe = make("vt_pe")
        self.vt_act = make("vt_act")
        self.idx_pe = make("idx_pe")
        self.idx_relu = make("idx_relu")
        self.idx_dve = make("idx_dve")
        self.topk = make("topk")
        self.conv_dve = make("conv_dve")
        self.conv_act = make("conv_act")
        self.xt_pe = make("xt_pe")
        self.xt_act = make("xt_act")
        self.cb_pe = make("cb_pe")
        self.cb_act = make("cb_act")
        self.ssd_bc = make("ssd_bc")
        self.ssd_em = make("ssd_em")
        self.ssd_w = make("ssd_w")
        self.ssd_m = make("ssd_m")
        self.ssd_y = make("ssd_y")
        self.ssd_dve = make("ssd_dve")
        self.ssd_z = make("ssd_z")
        self.ssd_sq = make("ssd_sq")
        self.gn_dve = make("gn_dve")
        self.gn_hi = make("gn_hi")
        self.gn_ready = make("gn_ready")
        self.out_landed = make("out_landed")


class HeadTiles:

    def __init__(self, take, k):
        self.q, self.k, self.v = take(f"l1_q{k}", T), take(f"l1_k{k}", T), take(f"l1_v{k}", T)
        self.gr, self.b = take(f"l1_gr{k}", T), take(f"l1_b{k}", T)
        self.xr, self.cx = take(f"l1_xr{k}", 260), take(f"l1_cx{k}", 260)


def program(nc, x, stream, gates, params, consts, onehot, table, bias_scratch, out):
    with ExitStack() as ctx:
        top = nc.sbuf_top
        base = (nc.sbuf_base + 63) // 64 * 64
        place = [base]

        def sb(name, words, dt=F32, at=None):
            off = place[0] if at is None else at
            t = nc.alloc_sbuf_tensor_at(name, [P, words], dt, offset=off)
            if at is None:
                place[0] = off + (4 * words + 31) // 32 * 32
                assert place[0] <= top, (name, place[0], top)
            return t[:, :], off

        def psum(name):
            return ctx.enter_context(nc.psum_tensor(name, [P, 512], F32))[:, :]

        raw = sb("raw", NSLOT * CW)[0].rearrange("p (s c) -> p s c", s=NSLOT)
        whi = sb("whi", NSLOT * CW, F32R)[0].rearrange("p (s c) -> p s c", s=NSLOT)
        wlo = sb("wlo", NSLOT * CW, F32R)[0].rearrange("p (s c) -> p s c", s=NSLOT)
        xT = sb("xT", DT * T)[0].rearrange("p (m t) -> p m t", t=T)
        a_hi = sb("a_hi", DT * T, F32R)[0].rearrange("p (m t) -> p m t", t=T)
        a_lo = sb("a_lo", DT * T, F32R)[0].rearrange("p (m t) -> p m t", t=T)
        b_hi_f, at_b = sb("b_hi", DT * T, F32R)
        b_lo_f, _ = sb("b_lo", DT * T, F32R)
        b_hi = b_hi_f.rearrange("p (m t) -> p m t", t=T)
        b_lo = b_lo_f.rearrange("p (m t) -> p m t", t=T)
        br_f, at_br = sb("branches", 12288, F32R)
        br = br_f.rearrange("p (r h m t) -> p r h m t", r=3, h=2, t=T)

        def under(start, words):
            place2 = [start]

            def take(name, n):
                t = sb(name, n, F32, at=place2[0])[0]
                place2[0] += (4 * n + 31) // 32 * 32
                assert place2[0] <= start + 4 * words, name
                return t
            return take

        par = sb("par", N_PARAMS)[0]
        cst = sb("cst", 384)[0]
        ident, ones = cst[:, 0:128], cst[:, 128:256]
        tril = cst[:, 256:384]
        par2 = sb("par2", 96)[0]
        m4sp, ba2, bx2 = par2[:, 0:8], par2[:, 8:16], par2[:, 16:24]
        nlam, gb2, a_exp = par2[:, 24:32], par2[:, 32:80], par2[:, 80:81]
        convh = sb("convh", 60)[0]
        rB = sb("rB", T)[0]
        rn = sb("rn", 3 * T)[0].rearrange("p (k t) -> p k t", t=T)
        sqacc = sb("sqacc", 2 * T)[0].rearrange("p (k t) -> p k t", t=T)
        sq = sb("sq", 2 * T)[0].rearrange("p (k t) -> p k t", t=T)
        t1 = sb("t1", T)[0]
        t2 = sb("t2", T)[0]
        L = sb("L", 384)[0]
        PTs = sb("PTs", 384)[0]
        small = sb("small", 8)[0]
        nmx, den, rden = small[:, 0:2], small[:, 2:4], small[:, 4:6]
        wk = sb("wk", 9 * T)[0].rearrange("p (k t) -> p k t", t=T)

        take = under(at_b, 8192)
        l1 = [HeadTiles(take, k) for k in range(2)]
        l1_c = take("l1_c", T)
        U = take("bias", HEADS * T).rearrange("p (h t) -> p h t", t=T)
        wg = take("wg", 2 * T).rearrange("p (h t) -> p h t", t=T)
        gth = sb("gth", 6 * T)[0].rearrange("p (k t) -> p k t", t=T)
        vtok = gth[:, 5, :]
        v_st, xt_st, xs_st, col_st = gth[:, 0, :], gth[:, 1, :], gth[:, 2, :], gth[:, 3, 0:2]
        take = under(at_br, 12288)
        oh = take("oh", 512)
        tab = take("tab", 8)
        brow = take("brow", HEADS * 512).rearrange("p (k c) -> p k c", k=HEADS)
        take = under(at_br, 12288)
        kN = take("kN", 4 * T).rearrange("p (k t) -> p k t", t=T)
        vtk = take("vtk", 4 * T).rearrange("p (k t) -> p k t", t=T)
        xs = take("xs", 8 * T).rearrange("p (k t) -> p k t", t=T)
        xtok = take("xtok", 2 * 1024).rearrange("p (s c) -> p s c", s=2)
        bc = take("bc", 4 * T).rearrange("p (k t) -> p k t", t=T)
        cbt = take("cbt", 2 * 384).rearrange("p (k t) -> p k t", k=2)
        score = take("score", 384)
        yz = xs
        qN = take("qN", 2 * T).rearrange("p (k t) -> p k t", t=T)
        qraw = take("qraw", 2 * T).rearrange("p (k t) -> p k t", t=T)
        zraw = take("zraw", 2 * T).rearrange("p (k t) -> p k t", t=T)
        sm_t = take("sm_t", T)
        kibd = take("kibd", 2 * T)
        dtA = take("dtA", 2 * T).rearrange("p (k t) -> p k t", k=2)
        r1B = take("r1B", T)
        causal = take("causal", 384)
        cbuf = take("cbuf", 260)
        tok = take("tok", 128)
        wi_tok = tok[:, 0:32].rearrange("p (s h) -> p s h", s=2)
        dt_tok = tok[:, 32:64].rearrange("p (s h) -> p s h", s=2)
        nA_tok = tok[:, 64:112].rearrange("p (s h) -> p s h", s=3)
        mx8 = tok[:, 112:128]

        acc = [psum("acc0"), psum("acc1")]
        pS, pT, pV, pO, pG, pN = (psum(n) for n in ("pS", "pT", "pV", "pO", "pG", "pN"))

        s = Semaphores(lambda name: ctx.enter_context(nc.semaphore(name)))
        landed = [ctx.enter_context(nc.semaphore(f"landed{k}")) for k in range(NSLOT)]
        wg_landed = [ctx.enter_context(nc.semaphore(f"wg_landed{k}")) for k in range(2)]
        bias_out = [ctx.enter_context(nc.semaphore(f"bias_out{k}")) for k in range(2)]

        def pcol(name, k=0):
            o = PARAMS[name]
            return par[:, ds(k.value(o), 1)] if isinstance(k, At) else par[:, o + k:o + k + 1]

        def apart(eng):
            eng.nop(nofuse=True)

        def tile(buf, m):
            return buf[:, ds(m.value(), 1), :].rearrange("p a t -> p (a t)")

        def lagged(eng, body):
            body(At(0), False)
            body(At(1), True)
            with eng.Fori(0, 3) as i:
                body(At(2, (i, 2)), True)
                body(At(3, (i, 2)), True)

        R = slice(DT_ROW, DT_ROW + 16)
        block = ctx.enter_context(nc.Block())

        @block.sync
        def _(sp):
            def load(c, slot):
                sp.dma_start(raw[:, slot, :], stream[ds(c, 1)].rearrange("a p c -> (a p) c")).then_inc(landed[slot], 16)

            sp.dma_start(par, params).then_inc(s.par_landed, 16)
            sp.dma_start(xT[:, 0:8, :], x[:, 0:8, :]).then_inc(s.x_landed, 16)
            load(0, 0)
            sp.dma_start(xT[:, 8:16, :], x[:, 8:16, :]).then_inc(s.x_landed2, 16)
            for c in range(1, NSLOT):
                load(c, c)
            sp.dma_start(cst, consts[:, 0:384]).then_inc(s.cst_landed, 16)
            sp.dma_start(oh[0:33, :], onehot).then_inc(s.oh_landed, 16)
            sp.dma_start(tab[0:33, :], table).then_inc(s.tab_landed, 16)
            whole = CHUNKS // NSLOT
            with sp.Fori(1, whole) as i:
                for k in range(NSLOT):
                    sp.wait_ge(s.lo_done, i * NSLOT + (k - NSLOT + 1))
                    load(i * NSLOT + k, k)
            for c in range(whole * NSLOT, CHUNKS):
                sp.wait_ge(s.lo_done, c - NSLOT + 1)
                load(c, c % NSLOT)

        @block.gpsimd
        def _(pool):
            nc.gpsimd.memset(sqacc.rearrange("p k t -> p (k t)"), 0.0).then_inc(s.pads, 1)
            for k in range(2):
                nc.gpsimd.memset(l1[k].xr[:, 0:3], 0.0)
                last = nc.gpsimd.memset(l1[k].cx[:, 0:2], 0.0)
            last.then_inc(s.pads, 1)
            for h in range(HEADS):
                pool.wait_ge(s.bias_copied, h + 1)
                pool.dma_start(bias_scratch[h, 0:P * 512].rearrange("(p c) -> p c", p=P),
                               brow[:, h, :]).then_inc(bias_out[h % 2], 16)
            for k in range(2):
                pool.wait_ge(bias_out[k], 16 * HEADS // 2)
            for h in range(HEADS):
                pool.dma_start(U[:, h, :], bias_scratch[h, 128:128 + P * 511].rearrange("(p c) -> p c", c=511)[:, 0:T])\
                    .then_inc(s.bias_in, 16)
            for k in range(2):
                pool.dma_start(wg[:, k, :], gates[:, T * k:T * k + T]).then_inc(wg_landed[k], 16)
            with pool.Fori(1, 4) as i:
                for k in range(2):
                    pool.wait_ge(s.lru_pe, i * 2 + (k - 1))
                    pool.dma_start(wg[:, k, :], gates[:, ds(i * (2 * T) + T * k, T)]).then_inc(wg_landed[k], 16)
            pool.wait_ge(s.evacuated, A_MLP1)
            pool.dma_start(causal, consts[:, 384:768]).then_inc(s.causal_landed, 16)
            nc.gpsimd.memset(kibd, 0.0)
            nc.gpsimd.memset(dtA.rearrange("p k t -> p (k t)"), 0.0)
            nc.gpsimd.memset(score, 0.0)
            nc.gpsimd.memset(cbuf, 0.0).then_inc(s.cleared, 1)
            COPY = nc.gpsimd.tensor_copy

            def stage_xs(i):
                pool.wait_ge(s.conv_dve, i.times(5).value(25))
                if i.least() > 0:
                    pool.wait_ge(s.xs_staged, i.value())
                    pool.wait_ge(s.xt_pe, i.value())
                apart(pool)
                COPY(xs_st, tile(xs, i)).then_inc(s.xs_staged, 1)

            stage_xs(At(0))
            with pool.Fori(0, 7) as i:
                stage_xs(At(1, (i, 1)))

            def stage_round(t):
                g, h = t.mod(2), t.div(2)
                if t.least() > 0:
                    pool.wait_ge(s.staged, t.value())
                    pool.wait_ge(s.pv_done, t.value(8))
                    pool.wait_ge(s.ssd_y, t.value())
                apart(pool)
                COPY(v_st, tile(vtk, h))
                COPY(xt_st.rearrange("p (s c) -> p s c", s=2), xtok[:, :, ds(h.times(128).value(512 * g), 128)])
                COPY(col_st, ident[:, ds(h.times(2).value(8 * g + DT_ROW), 2)]).then_inc(s.staged, 1)

            pool.wait_ge(s.vt_act, 4)
            pool.wait_ge(s.xt_act, 8)
            def add_square(t):
                pool.wait_ge(s.ssd_sq, t.value(1))
                if t.least() > 0:
                    pool.wait_ge(s.ssd_sum, t.value())
                acc_sq = sqacc[:, t.mod(2), :]
                nc.gpsimd.tensor_tensor(acc_sq, acc_sq, sq[:, 1, :], ALU.add).then_inc(s.ssd_sum, 1)

            stage_round(At(0))
            for t in (At(1), At(2)):
                stage_round(t)
                add_square(t.plus(-1))
            with pool.Fori(0, 2) as i:
                for k in range(2):
                    stage_round(At(3 + k, (i, 2)))
                    add_square(At(2 + k, (i, 2)))
            stage_round(At(7))
            add_square(At(6))
            add_square(At(7))

        @block.scalar
        def _(act):
            A = nc.scalar.activation

            def prep(c):
                c = c.plus(LEAD)
                if c.least() >= CHUNKS:
                    return
                slot = c.mod(NSLOT)
                act.wait_ge(landed[slot], c.div(NSLOT).times(16).value(16))
                if c.least() >= NSLOT:
                    act.wait_ge(s.mm_done, c.value(1 - NSLOT))
                A(whi[:, slot, :], raw[:, slot, :], ACT.Copy).then_inc(s.hi_done, 1)

            def square_buffer(n):
                if n.least() >= 2:
                    act.wait_ge(s.sq_added, n.value(-1))

            def norm_in(stage, m, gain, a):
                n = m.plus(16 * stage)
                if a is not None:
                    act.wait_ge(s.evacuated, a.value(1))
                    apart(act)
                A(tile(a_hi, m), tile(xT, m), ACT.Copy, scale=pcol(gain, m)).then_inc(s.a_hi_ready, 1)
                square_buffer(n)
                apart(act)
                A(sq[:, n.mod(2), :], tile(xT, m), ACT.Square).then_inc(s.sq_ready, 1)

            def std(n, rows=P):
                act.wait_ge(s.var_ready, n.value(1))
                A(rn[0:rows, 1, :], rn[0:rows, 0, :], ACT.Ln).then_inc(s.std_ready, 1)
                act.wait_ge(s.std_ready, n.times(2).value(1))
                A(rn[0:rows, 1, :], rn[0:rows, 1, :], ACT.Exp, scale=-0.5).then_inc(s.std_ready, 1)

            def attn_exp(n):
                act.wait_ge(s.nmax_ready, n.value(1))
                A(L[:, 0:128], L[:, 0:128], ACT.Exp, bias=nmx[:, 0:1], accum_out=den[:, 0:1])
                A(L[:, 128:384], L[:, 128:384], ACT.Exp, bias=nmx[:, 1:2], accum_out=den[:, 1:2]).then_inc(s.probs_exp, 1)

            def attn_pt(n):
                act.wait_ge(s.probs_transposed, n.value(1))
                if n.least() > 0:
                    act.wait_ge(s.pv_done, n.value())
                A(PTs, pT[:, 0:384], ACT.Copy).then_inc(s.pt_copied, 1)

            def attn_v(n):
                act.wait_ge(s.v_transposed, n.value(1))
                if n.least() > 0:
                    act.wait_ge(s.pv_done, n.value())
                A(vtok, pV[:, 0:T], ACT.Copy).then_inc(s.v_copied, 1)

            def attn_hi(n, dst):
                act.wait_ge(s.pv_done, n.value(1))
                apart(act)
                A(dst, pO[:, 0:T], ACT.Copy).then_inc(s.attn_hi, 1)

            def side1(j, t):
                lru = Steps(act, s.lru_act, 8, t)
                lru_d = Steps(act, s.lru_dve, 15, t)
                if j == 1:
                    attn_exp(t)
                    attn_v(t)
                if j == 2:
                    act.wait_ge(s.lru_pe, t.value(1))
                    apart(act)
                    lru.step(A(wk[:, 1, :], pG[:, 0:T], ACT.Tanh, bias=ba2[:, ds(t.value(), 1)], scale=0.5))
                    lru.step(A(wk[:, 2, :], pG[:, T:2 * T], ACT.Tanh, bias=bx2[:, ds(t.value(), 1)], scale=0.5))
                if j == 3:
                    attn_pt(t)
                    lru.k = 2
                    lru_d.wait(5)
                    lru.step(A(wk[:, 4, :], wk[:, 3, :], ACT.Exp))
                    lru.step(A(wk[:, 5, :], wk[:, 3, :], ACT.Exp, scale=2.0))
                    lru.step(A(wk[:, 6, :], wk[:, 3, :], ACT.Tanh, scale=-1.0))
                if j == 4:
                    attn_hi(t, tile(br[:, 0, 0], t))
                if j == 5:
                    lru.k = 5
                    lru_d.wait(7)
                    lru.step(A(wk[:, 5, :], wk[:, 6, :], ACT.Sqrt))
                if j == 6:
                    lru.k = 6
                    lru_d.wait(10)
                    lru_d.wait(11)
                    lru.step(A(wk[:, 5, :], wk[:, 1, :], ACT.Tanh))
                if j == 7:
                    lru.k = 7
                    Steps(act, s.sc_dve, 5, t).wait(4)
                    apart(act)
                    A(tile(br[:, 2, 0], t), wk[:, 8, :], ACT.Copy).then_inc(s.sc_act, 1)
                    lru_d.wait(14)
                    apart(act)
                    lru.step(A(tile(br[:, 1, 0], t), wk[:, 7, :], ACT.Copy))

            act.wait_ge(s.par_landed, 16)
            act.wait_ge(s.x_landed, 16)
            for m in range(DT):
                if m == 8:
                    act.wait_ge(s.x_landed2, 16)
                norm_in(0, At(m), "g_mix1", None)
                if m in (5, 7, 9, 11):
                    prep(At((m - 5) // 2 - LEAD))
            A(ba2, par[:, PARAMS["lru_ba"]:PARAMS["lru_ba"] + 8], ACT.Copy, scale=0.5)
            A(bx2, par[:, PARAMS["lru_bx"]:PARAMS["lru_bx"] + 8], ACT.Copy, scale=0.5)
            A(gb2, par[:, PARAMS["gate_b"]:PARAMS["gate_b"] + 48], ACT.Copy, scale=0.5)
            A(convh, par[:, PARAMS["conv_w"]:PARAMS["conv_w"] + 60], ACT.Copy, scale=0.5)
            A(a_exp, pcol("a_log"), ACT.Exp).then_inc(s.setup_act, 1)
            act.wait_ge(s.setup_act, 1)
            act.wait_ge(s.sp_dve, 2)
            A(rn[:, 1, 0:8], rn[:, 0, 0:8], ACT.Exp).then_inc(s.sp_act, 1)

            def bias_rows(j):
                for h in (2 * j, 2 * j + 1):
                    act.wait_ge(s.bias_ps, h + 1)
                    A(brow[:, h, :], (pG if h % 2 else pO)[:, 0:512], ACT.Copy).then_inc(s.bias_copied, 1)

            def tile1(i, side):
                for j in range(8):
                    c = i.times(16).plus(2 * j)
                    if i.base == 0 and 1 <= j <= 4:
                        bias_rows(j - 1)
                    prep(c)
                    if i.base == 0 and j == 0:
                        std(At(0))
                    if side:
                        side1(j, i.plus(-1))
                    prep(c.plus(1))

            lagged(act, tile1)

            def mix(q, side):
                for h in range(2):
                    c = q.times(36).plus(B_Y + 18 * h)
                    for j in range(6):
                        prep(c.plus(2 * j))
                        if side and h == 0:
                            side1(j, At(7))
                        prep(c.plus(2 * j + 1))
                        act.wait_ge(s.evacuated, q.times(24).plus(A_Y + 12 * h + j).value(1))
                        apart(act)
                        b = q.times(4).plus(2 * h + j // 3 + 16 * (j % 3))
                        A(gth[:, j, :], gth[:, j, :], ACT.Tanh, bias=gb2[:, ds(b.value(), 1)], scale=0.5).then_inc(s.gate_th, 1)
                    if side and h == 0:
                        side1(6, At(7))
                        side1(7, At(7))
                    for k in range(2):
                        m = q.times(4).plus(2 * h + k)
                        for n in range(3):
                            prep(c.plus(12 + 3 * k + n))
                        act.wait_ge(s.mix_dve, m.times(2).value(2))
                        apart(act)
                        A(tile(b_hi, m), t2, ACT.Copy, scale=0.5).then_inc(s.mix_hi, 1)

            mix(At(0), True)
            with act.Fori(1, 4) as q:
                mix(At(0, (q, 1)), False)

            def out_tiles(b, a, stage, gain):
                with act.Fori(0, 8) as i:
                    for k in range(2):
                        c = At(b + 2 * k, (i, 4))
                        prep(c)
                        prep(c.plus(1))
                        norm_in(stage, At(k, (i, 2)), gain, At(a + k, (i, 2)))

            out_tiles(B_OUT1, A_OUT1, 1, "g_mlp1")

            def mlp(b, a, layer, norm):
                for g in range(FF_GROUPS):
                    def up(m):
                        n = m.plus(64 * layer + 16 * g)
                        c = m.times(2).plus(b + 64 * g)
                        prep(c)
                        if g == 0 and m.base == 0 and not m.terms:
                            std(At(norm))
                        prep(c.plus(1))
                        act.wait_ge(s.up_dve, n.times(2).value(2))
                        apart(act)
                        A(tile(b_hi, m), t2, ACT.Copy).then_inc(s.hid_hi, 1)

                    def down(m):
                        c = m.times(2).plus(b + 64 * g + 32)
                        prep(c)
                        prep(c.plus(1))
                        if g == FF_GROUPS - 1:
                            e = m.plus(a + 32 * g + 16)
                            if layer == 0:
                                fin1(m, e)
                            else:
                                act.wait_ge(s.evacuated, e.value(1))
                                act.dma_start(out[:, ds(m.value(), 1), :].rearrange("p a t -> p (a t)"), tile(xT, m)).then_inc(s.out_landed, 16)

                    up(At(0))
                    up(At(1))
                    with act.Fori(1, 8) as j:
                        up(At(0, (j, 2)))
                        up(At(1, (j, 2)))
                    with act.Fori(0, 7) as j:
                        down(At(0, (j, 2)))
                        down(At(1, (j, 2)))
                    down(At(14))
                    down(At(15))

            def fin1(m, e):
                act.wait_ge(s.evacuated, e.value(1))
                act.wait_ge(s.sq_added, m.value(32))
                apart(act)
                A(sq[:, 0, :], tile(xT, m), ACT.Square)
                A(tile(xT, m), tile(xT, m), ACT.Copy, scale=pcol("final_g", m)).then_inc(s.fin_act, 1)
                act.wait_ge(s.fin_act, m.value(1))
                apart(act)
                A(tile(a_hi, m), tile(xT, m), ACT.Copy, scale=pcol("g_mix2", m)).then_inc(s.a_hi_ready, 1)
                A(sq[:, 1, :], tile(xT, m), ACT.Square).then_inc(s.sq_ready, 1)

            mlp(B_MLP1, A_MLP1, 0, 1)

            def head_sq(n, src, a, rows=P):
                act.wait_ge(s.evacuated, a.value(1))
                act.wait_ge(s.stat_ready, n.value(4))
                A(sq[0:rows, 0, :], src[0:rows], ACT.Square).then_inc(s.nh_sq, 1)

            c = At(B_L2)
            prep(c)
            std(At(2))
            std(At(3))
            prep(c.plus(1))
            head_sq(At(0), sm_t, At(A_L2), 64)

            for k in range(4):
                c = At(B_L2 + 2 + 2 * k)
                prep(c)
                prep(c.plus(1))
                if k == 0:
                    act.wait_ge(s.sp_dve, 16 + 2)
                    A(rn[R, 1, :], rn[R, 0, :], ACT.Exp).then_inc(s.sp_act, 1)
                    act.wait_ge(s.sm_pe, 1)
                    A(wi_tok[:, 0, :], pV[:, WI_COL:WI_COL + 16], ACT.Copy, scale=1.0 / 32.0)
                    A(wi_tok[:, 1, :], pV[:, 128 + WI_COL:128 + WI_COL + 16], ACT.Copy, scale=1.0 / 32.0).then_inc(s.sm_act, 1)
                if k == 3:
                    act.wait_ge(s.sm_pe, 2)
                    for h in range(2):
                        A(dt_tok[:, h, :], pT[:, 128 * h + DT_ROW:128 * h + DT_ROW + 16], ACT.Copy)
                        last = A(nA_tok[:, 2 * h, :], pT[:, 256 + 128 * h + DT_ROW:256 + 128 * h + DT_ROW + 16], ACT.Copy, scale=-1.0)
                    last.then_inc(s.sm_act, 1)
                std(At(4 + k), 64 if k == 0 else P)
                if k == 1:
                    act.wait_ge(s.nh_ready, 1)
                    act.wait_ge(s.cleared, 1)
                    act.dma_start(kibd[64:128, T:2 * T], kibd[0:64, 0:T]).then_inc(s.sm_dma, 16)
                head_sq(At(1 + k), qraw[:, (1 + k) % 2, :], At(A_L2 + 1 + k))

            def v_copy(n):
                act.wait_ge(s.vt_pe, n.value(1))
                A(tile(vtk, n), pV[:, 0:T], ACT.Copy).then_inc(s.vt_act, 1)

            for k in range(4):
                c = At(B_L2 + 10 + 2 * k)
                prep(c)
                prep(c.plus(1))
                if k == 0:
                    std(At(8))
                v_copy(At(k))

            def idx_relu(n):
                act.wait_ge(s.idx_pe, n.value(1))
                if n.least() > 0:
                    act.wait_ge(s.idx_dve, n.times(4).value())
                A(wk[:, 0, :], pT[:, 0:T], ACT.Relu)
                A(wk[:, 1:3, :].rearrange("p k t -> p (k t)"), pS[:, 0:2 * T], ACT.Relu).then_inc(s.idx_relu, 1)

            def tile_qi(i, side):
                c = i.times(2).plus(B_L2 + 18)
                prep(c)
                if side:
                    idx_relu(i.plus(-1))
                prep(c.plus(1))

            lagged(act, tile_qi)

            def conv_tanh(n):
                act.wait_ge(s.conv_dve, n.times(5).value(4))
                A(wk[:, 4, :], wk[:, 3, :], ACT.Tanh).then_inc(s.conv_act, 1)

            for n in range(4):
                c = At(B_L2 + 34 + 2 * n)
                prep(c)
                if n == 0:
                    idx_relu(At(7))
                prep(c.plus(1))
                conv_tanh(At(n))

            def xs_copy(n):
                act.wait_ge(s.xt_pe, n.value(1))
                apart(act)
                A(xtok[:, :, ds(n.times(128).value(), 128)], pV[:, 0:T].rearrange("p (s c) -> p s c", s=2), ACT.Copy)\
                    .then_inc(s.xt_act, 1)

            def tile_xs(i, side):
                c = i.times(2).plus(B_L2 + 42)
                prep(c)
                if side:
                    xs_copy(i.plus(-1))
                else:
                    act.wait_ge(s.cb_pe, 1)
                    A(cbt[:, 0, :], pG[:, 0:384], ACT.Copy)
                    A(cbt[:, 1, :], pO[:, 0:384], ACT.Copy).then_inc(s.cb_act, 1)
                prep(c.plus(1))
                conv_tanh(i.plus(4))

            lagged(act, tile_xs)

            W = wk[:, 2:5, :].rearrange("p k t -> p (k t)")

            def ssd_exp(t):
                act.wait_ge(s.ssd_em, t.value(1))
                apart(act)
                for h in range(2):
                    n = t.div(2).times(2).plus(8 * t.mod(2) + h)
                    w = W[:, 384 * h:384 * h + 384]
                    A(w[:, 0:128], wk[:, h, 0:128], ACT.Exp, bias=nA_tok[:, 0, ds(n.value(), 1)])
                    A(w[:, 128:256], pG[:, 256 * h + 128:256 * h + 256], ACT.Exp, bias=nA_tok[:, 1, ds(n.value(), 1)])
                    last = A(w[:, 256:384], wk[:, h, 128:256], ACT.Exp, bias=nA_tok[:, 2, ds(n.value(), 1)])
                last.then_inc(s.ssd_w, 1)
                A(wk[:, 5, :], zraw[:, t.mod(2), :], ACT.Tanh, scale=0.5).then_inc(s.ssd_z, 1)

            def side2(j, t):
                n = t.plus(8)
                if j == 0:
                    attn_exp(n)
                if j == 1:
                    ssd_exp(t)
                if j == 2:
                    attn_pt(n)
                if j == 3:
                    attn_hi(n, tile(b_hi, n))
                    act.wait_ge(s.ssd_dve, t.times(3).value(3))
                    if t.least() > 0:
                        act.wait_ge(s.ssd_sum, t.value())
                    apart(act)
                    A(sq[:, 1, :], tile(yz, t.div(2).plus(4 * t.mod(2))), ACT.Square).then_inc(s.ssd_sq, 1)

            def tile_qz(i, side):
                c = i.times(4).plus(B_L2 + 58)
                for j in range(4):
                    prep(c.plus(j))
                    if not side and j == 0:
                        xs_copy(At(7))
                    if side and j < 3:
                        side2(j, i.plus(-1))
                    if j == 1:
                        head_sq(i.plus(5), qraw[:, i.mod(2), :], i.times(2).plus(A_L2 + 29))
                    if j == 3:
                        std(i.plus(9))
                        if side:
                            side2(3, i.plus(-1))

            lagged(act, tile_qz)
            for j in range(4):
                side2(j, At(7))
            for g in range(2):
                std(At(17 + g))
            for m in range(8):
                act.wait_ge(s.gn_dve, m + 1)
                A(b_hi[:, m, :], yz[:, m, :], ACT.Copy).then_inc(s.gn_hi, 1)
            out_tiles(B_OUT2, A_OUT2, 3, "g_mlp2")
            mlp(B_MLP2, A_MLP2, 1, 19)
            act.wait_ge(s.out_landed, 16 * DT)

        @block.vector
        def _(dve):
            V = nc.vector
            STT, TT, TS = V.scalar_tensor_tensor, V.tensor_tensor, V.tensor_scalar
            MUL, ADD, SUB, MAX, MIN = ALU.mult, ALU.add, ALU.subtract, ALU.max, ALU.min

            def prep(c):
                c = c.plus(LEAD)
                if c.least() >= CHUNKS:
                    return
                slot = c.mod(NSLOT)
                dve.wait_ge(s.hi_done, c.value(1))
                TT(wlo[:, slot, :], raw[:, slot, :], whi[:, slot, :].bitcast(F32), SUB).then_inc(s.lo_done, 1)

            def acc_wait(c):
                dve.wait_ge(s.mm_done, c.value(1))

            def evac(c, a, dst, scale=rB, rows=slice(0, P)):
                acc_wait(c)
                TT(dst, acc[a.mod(2)][rows, 0:T], scale[rows], MUL).then_inc(s.evacuated, 1)

            def norm_lo(stage, m, gain, k=1):
                n = m.plus(16 * stage)
                dve.wait_ge(s.a_hi_ready, n.value(1))
                STT(tile(a_lo, m), tile(xT, m), pcol(gain, m), tile(a_hi, m).bitcast(F32), MUL, SUB).then_inc(s.a_ready, 1)
                dve.wait_ge(s.sq_ready, n.value(1))
                if n.least() > 0:
                    dve.wait_ge(s.sq_added, n.value())
                b = n.mod(2) if k == 1 else 0
                TT(sqacc[:, 0:k, :], sqacc[:, 0:k, :], sq[:, b:b + k, :], ADD).then_inc(s.sq_added, 1)

            def rsqrt(n, scale, dst, rows=P, src=None):
                st = Steps(dve, s.r_steps, 4, n)
                v, y, w = rn[0:rows, 0, :], rn[0:rows, 1, :], rn[0:rows, 2, :]
                if src is None:
                    dve.wait_ge(s.stat_ready, n.value(1))
                    src = pN[0:rows, 0:T]
                TS(v, src, scale, EPS, MUL, ADD).then_inc(s.var_ready, 1)
                dve.wait_ge(s.std_ready, n.times(2).value(2))
                st.step(TT(w, v, y, MUL))
                st.wait()
                st.step(TT(w, w, y, MUL))
                st.wait()
                st.step(TS(w, w, -0.5, 1.5, MUL, ADD))
                st.wait()
                st.step(TT(dst, w, y, MUL))
                st.wait()

            def clear_sums(n):
                V.memset(sqacc.rearrange("p k t -> p (k t)"), 0.0).then_inc(s.sq_zeroed, 1)
                dve.wait_ge(s.sq_zeroed, n)

            def softplus(dst, src, n, tmp):
                st = Steps(dve, s.sp_dve, 16, At(n))
                st.k = 1
                st.wait()
                x0, x1, x2 = (tmp(k) for k in range(3))
                st.step(STT(x0, src, -1.0, src, MUL, MIN))
                st.wait()
                dve.wait_ge(s.sp_act, n + 1)
                st.step(TS(x0, x1, 2.0, None, ADD))
                st.wait()
                st.step(V.reciprocal(x0, x0))
                st.wait()
                st.step(TT(x1, x1, x0, MUL))
                st.wait()
                st.step(TT(x0, x1, x1, MUL))
                st.wait()
                st.step(TS(x2, x0, 1.0 / 15.0, None, MUL))
                for k in (13, 11, 9, 7, 5, 3):
                    st.wait()
                    st.step(STT(x2, x2, 1.0 / k, x0, ADD, MUL))
                st.wait()
                st.step(STT(x2, x2, 1.0, x1, ADD, MUL))
                st.wait()
                st.step(TS(x2, x2, 2.0, None, MUL))
                st.wait()
                st.step(STT(dst, src, 0.0, x2, MAX, ADD))
                st.wait()

            def attn_logits(n, b0, b1):
                dve.wait_ge(s.scores_ready, n.value(1))
                if n.least() > 0:
                    dve.wait_ge(s.probs_transposed, n.value())
                STT(L[:, 0:128], pS[:, 0:128], QK_SCALE, b0, MUL, ADD)
                STT(L[:, 128:384], pS[:, 128:384], QK_SCALE, b1, MUL, ADD).then_inc(s.logits_ready, 1)
                dve.wait_ge(s.logits_ready, n.value(1))
                V.tensor_reduce(nmx[:, 0:1], L[:, 0:128], AX_X, MAX, negate=True)
                V.tensor_reduce(nmx[:, 1:2], L[:, 128:384], AX_X, MAX, negate=True).then_inc(s.nmax_ready, 1)

            def attn_norm(n):
                dve.wait_ge(s.probs_exp, n.value(1))
                V.reciprocal(rden, den).then_inc(s.den_inv, 1)
                dve.wait_ge(s.den_inv, n.value(1))
                TS(L[:, 0:128], L[:, 0:128], rden[:, 0:1], None, MUL)
                TS(L[:, 128:384], L[:, 128:384], rden[:, 1:2], None, MUL).then_inc(s.probs_ready, 1)

            def attn_lo(n, dst, hi):
                dve.wait_ge(s.attn_hi, n.value(1))
                TT(dst, pO[:, 0:T], hi.bitcast(F32), SUB).then_inc(s.attn_ready, 1)

            def side1(j, t, p):
                lru = Steps(dve, s.lru_dve, 15, t)
                lru_a = Steps(dve, s.lru_act, 8, t)
                sc = Steps(dve, s.sc_dve, 5, t)
                b = l1[p]
                if j == 0:
                    dve.wait_ge(s.evacuated, t.times(8).value(8))
                    lru.step(TS(wk[:, 0, :], b.xr[:, 3:3 + T], pcol("lru_w", t.plus(24)), pcol("lru_b", t), MUL, ADD))
                    for k in range(3):
                        lru.wait()
                        lru.step(STT(wk[:, 0, :], b.xr[:, k:k + T], pcol("lru_w", t.plus(8 * k)), wk[:, 0, :], MUL, ADD))
                if j == 1:
                    if t.base == 0:
                        dve.wait_ge(s.bias_in, 16 * HEADS)
                    u = tile(U, t)
                    attn_logits(t, u[:, 128:T], u)
                    sc.step(TS(wk[:, 8, :], b.cx[:, 0:T], pcol("sc_w", t), None, MUL))
                    for k in (1, 2):
                        sc.wait()
                        sc.step(STT(wk[:, 8, :], b.cx[:, k:k + T], pcol("sc_w", t.plus(8 * k)), wk[:, 8, :], MUL, ADD))
                    sc.wait()
                    sc.step(TT(wk[:, 8, :], wk[:, 8, :], b.b, MUL))
                if j == 2:
                    attn_norm(t)
                if j == 3:
                    lru.k = 4
                    lru_a.wait(2)
                    lru.step(TS(wk[:, 3, :], wk[:, 1, :], 1.0, m4sp[:, ds(t.value(), 1)], ADD, MUL))
                    lru.step(STT(wk[:, 2, :], wk[:, 2, :], 1.0, wk[:, 0, :], ADD, MUL))
                if j == 4:
                    lru.k = 6
                    lru_a.wait(5)
                    lru.step(STT(wk[:, 6, :], wk[:, 5, :], 1.0, wk[:, 6, :], ADD, MUL))
                if j == 5:
                    lru.k = 7
                    lru.step(TT(wk[:, 1, :], b.gr, b.gr, MUL))
                    lru.wait()
                    lru.step(TS(wk[:, 1, :], wk[:, 1, :], GELU_C1, GELU_C0, MUL, ADD))
                    lru.wait()
                    lru.step(TT(wk[:, 1, :], wk[:, 1, :], b.gr, MUL))
                    attn_lo(t, tile(br[:, 0, 1], t), tile(br[:, 0, 0], t))
                if j == 6:
                    lru.k = 10
                    lru_a.wait(6)
                    lru.step(STT(wk[:, 2, :], wk[:, 2, :], 0.5, wk[:, 5, :], MUL, MUL))
                    lru.wait()
                    lru.step(V.tensor_tensor_scan(wk[:, 3, :], wk[:, 4, :], wk[:, 2, :], 0.0, MUL, ADD))
                if j == 7:
                    lru.k = 12
                    lru_a.wait(7)
                    lru.step(STT(wk[:, 5, :], wk[:, 5, :], 1.0, b.gr, ADD, MUL))
                    lru.wait()
                    lru.step(STT(wk[:, 7, :], wk[:, 5, :], 0.5, wk[:, 3, :], MUL, MUL))
                    sc.k = 4
                    dve.wait_ge(s.sc_act, t.value(1))
                    sc.step(TT(tile(br[:, 2, 1], t), wk[:, 8, :], tile(br[:, 2, 0], t).bitcast(F32), SUB))
                    lru_a.wait(8)
                    lru.step(TT(tile(br[:, 1, 1], t), wk[:, 7, :], tile(br[:, 1, 0], t).bitcast(F32), SUB))

            dve.wait_ge(s.pads, 1)
            for m in range(DT):
                norm_lo(0, At(m), "g_mix1")
                if m in (5, 7, 9, 11):
                    prep(At((m - 5) // 2 - LEAD))
            dve.wait_ge(s.pads, 2)
            TS(nlam, par[:, PARAMS["lam"]:PARAMS["lam"] + 8], -1.0, None, MUL).then_inc(s.sp_dve, 1)
            softplus(m4sp, nlam, 0, lambda k: rn[:, k, 0:8])
            TS(m4sp, m4sp, -4.0, None, MUL).then_inc(s.setup_dve, 1)
            dve.wait_ge(s.setup_dve, 1)

            def tile1(i, side):
                b = l1[i.mod(2)]
                for j in range(8):
                    c, a = i.times(16).plus(2 * j), i.times(8).plus(j)
                    prep(c)
                    if side:
                        side1(j, i.plus(-1), (i.base + 1) % 2)
                    if i.base == 0 and j == 0:
                        rsqrt(At(0), 1.0 / D, rB)
                    last = c.plus(1)
                    if j < 5:
                        evac(last, a, (b.q, b.k, b.v, b.xr[:, 3:3 + T], b.gr)[j])
                    elif j == 5:
                        evac(last, a, l1_c)
                    elif j == 6:
                        evac(last, a, t1)
                        dve.wait_ge(s.evacuated, a.value(1))
                        TT(b.cx[:, 2:2 + T], t1, l1_c, MUL)
                    else:
                        evac(last, a, b.b)
                    prep(c.plus(1))

            lagged(dve, tile1)

            def mix(q, side):
                for h in range(2):
                    c = q.times(36).plus(B_Y + 18 * h)
                    a = q.times(24).plus(A_Y + 12 * h)
                    for j in range(6):
                        prep(c.plus(2 * j))
                        if side and h == 0:
                            side1(j, At(7), 1)
                        evac(c.plus(2 * j + 1), a.plus(j), gth[:, j, :])
                        prep(c.plus(2 * j + 1))
                    if side and h == 0:
                        side1(6, At(7), 1)
                        side1(7, At(7), 1)
                    for k in range(2):
                        m = q.times(4).plus(2 * h + k)
                        st = Steps(dve, s.mix_dve, 2, m)
                        dve.wait_ge(s.gate_th, q.times(12).plus(6 * h + 3 * k + 3).value())
                        for n, g in enumerate((0, 2, 1)):
                            cn, an = c.plus(12 + 3 * k + n), a.plus(6 + 3 * k + n)
                            prep(cn)
                            acc_wait(cn)
                            dst = (t1, t2, t1)[n]
                            STT(dst, gth[:, 3 * k + g, :], 1.0, acc[an.mod(2)][:, 0:T], ADD, MUL).then_inc(s.evacuated, 1)
                            if n:
                                dve.wait_ge(s.evacuated, an.value(1))
                                st.step(TT(t2, t1, t2, ADD))
                                st.wait()
                        dve.wait_ge(s.mix_hi, m.value(1))
                        STT(tile(b_lo, m), t2, 0.5, tile(b_hi, m).bitcast(F32), MUL, SUB).then_inc(s.mix_ready, 1)
                        dve.wait_ge(s.mix_ready, m.value(1))

            mix(At(0), True)
            with dve.Fori(1, 4) as q:
                mix(At(0, (q, 1)), False)

            def out_tiles(b, a, stage, gain):
                with dve.Fori(0, 8) as i:
                    for k in range(2):
                        c, e, m = At(b + 2 * k, (i, 4)), At(a + k, (i, 2)), At(k, (i, 2))
                        prep(c)
                        if stage == 3:
                            TT(t1, tile(xT, m), r1B, MUL).then_inc(s.x2_dve, 1)
                            dve.wait_ge(s.x2_dve, m.value(4))
                        acc_wait(c.plus(1))
                        TT(tile(xT, m), t1 if stage == 3 else tile(xT, m), acc[e.mod(2)][:, 0:T], ADD).then_inc(s.evacuated, 1)
                        prep(c.plus(1))
                        norm_lo(stage, m, gain)

            clear_sums(1)
            out_tiles(B_OUT1, A_OUT1, 1, "g_mlp1")

            def mlp(b, a, layer, norm):
                for g in range(FF_GROUPS):
                    def up(m):
                        n = m.plus(64 * layer + 16 * g)
                        c, e = m.times(2).plus(b + 64 * g), m.plus(a + 32 * g)
                        st = Steps(dve, s.up_dve, 2, n)
                        prep(c)
                        if g == 0 and m.base == 0 and not m.terms:
                            rsqrt(At(norm), 1.0 / D, rB)
                            clear_sums(2 if layer == 0 else 5)
                        evac(c.plus(1), e, t1)
                        dve.wait_ge(s.evacuated, e.value(1))
                        st.k = 1
                        STT(t2, t1, 0.0, t1, MAX, MUL).then_inc(s.up_dve, 2)
                        prep(c.plus(1))
                        dve.wait_ge(s.hid_hi, n.value(1))
                        TT(tile(b_lo, m), t2, tile(b_hi, m).bitcast(F32), SUB).then_inc(s.hid_ready, 1)

                    def down(m):
                        c, e = m.times(2).plus(b + 64 * g + 32), m.plus(a + 32 * g + 16)
                        prep(c)
                        acc_wait(c.plus(1))
                        TT(tile(xT, m), tile(xT, m), acc[e.mod(2)][:, 0:T], ADD).then_inc(s.evacuated, 1)
                        prep(c.plus(1))
                        if g == FF_GROUPS - 1 and layer == 0:
                            norm_lo(2, m, "g_mix2", 2)

                    up(At(0))
                    up(At(1))
                    with dve.Fori(1, 8) as j:
                        up(At(0, (j, 2)))
                        up(At(1, (j, 2)))
                    with dve.Fori(0, 7) as j:
                        down(At(0, (j, 2)))
                        down(At(1, (j, 2)))
                    down(At(14))
                    down(At(15))

            mlp(B_MLP1, A_MLP1, 0, 1)

            c = At(B_L2)
            prep(c)
            dve.wait_ge(s.stat_ready, 4)
            rsqrt(At(2), 1.0 / D, r1B)
            TT(t1, pN[:, T:2 * T], r1B, MUL).then_inc(s.x2_dve, 1)
            dve.wait_ge(s.x2_dve, 1)
            TT(t2, t1, r1B, MUL).then_inc(s.x2_dve, 1)
            dve.wait_ge(s.x2_dve, 2)
            rsqrt(At(3), 1.0 / D, t1, src=t2)
            TT(rB, t1, r1B, MUL).then_inc(s.x2_dve, 1)
            dve.wait_ge(s.x2_dve, 3)
            clear_sums(3)
            evac(c.plus(1), At(A_L2), sm_t)
            prep(c.plus(1))
            dve.wait_ge(s.evacuated, A_L2 + 1)
            TS(sm_t[R], sm_t[R], pcol("dt_bias")[R], None, ADD).then_inc(s.sp_dve, 1)

            def head_norm(n, src, gain, dst, rows=P):
                rsqrt(n.plus(4), 1.0 / rows, t1[0:rows], rows)
                STT(dst, src, pcol(gain)[0:rows], t1[0:rows], MUL, MUL).then_inc(s.nh_ready, 1)
                dve.wait_ge(s.nh_ready, n.value(1))

            for k in range(4):
                c, a = At(B_L2 + 2 + 2 * k), At(A_L2 + 1 + k)
                prep(c)
                if k == 0:
                    dve.wait_ge(s.cleared, 1)
                    softplus(dtA[R, 0, :], sm_t[R], 1, lambda k: rn[R, k, :])
                    st = Steps(dve, s.sm_dve, 4, At(0))
                    st.step(TS(rn[R, 0, :], dtA[R, 0, :], a_exp[R], -1.0, MUL, MUL))
                    st.wait()
                    for h in range(2):
                        st.step(V.tensor_tensor_scan(dtA[R, 1, 128 * h:128 * h + 128], ones[R, :],
                                                     rn[R, 0, 128 * h:128 * h + 128], 0.0, MUL, ADD))
                    st.wait()
                evac(c.plus(1), a, qraw[:, (1 + k) % 2, :])
                prep(c.plus(1))
                if k == 0:
                    head_norm(At(0), sm_t[0:64], "g_kidx", kibd[0:64, 0:T], 64)
                else:
                    head_norm(At(k), qraw[:, k % 2, :], "g_k", kN[:, k - 1, :])
            for k in range(4):
                c, a = At(B_L2 + 10 + 2 * k), At(A_L2 + 5 + k)
                prep(c)
                evac(c.plus(1), a, qraw[:, (1 + k) % 2, :])
                prep(c.plus(1))
                if k == 0:
                    head_norm(At(4), qraw[:, 0, :], "g_k", kN[:, 3, :])
                    dve.wait_ge(s.sm_act, 2)
                    TT(nA_tok[:, 1, :], pS[:, 0:16], nA_tok[:, 0, :], ADD).then_inc(s.sm_dve, 1)

            def idx_add(n):
                dve.wait_ge(s.idx_relu, n.value(1))
                st = Steps(dve, s.idx_dve, 4, n)
                for h in range(2):
                    if h:
                        st.wait()
                    col = n.times(2).plus(h)
                    st.step(STT(score[:, 0:128], wk[:, 0, 128 * h:128 * h + 128], wi_tok[:, 0, ds(col.value(), 1)],
                                score[:, 0:128], MUL, ADD))
                    st.step(STT(score[:, 128:384], wk[:, 1 + h, :], wi_tok[:, 1, ds(col.value(), 1)],
                                score[:, 128:384], MUL, ADD))
                st.wait()

            def tile_qi(i, side):
                c, a = i.times(2).plus(B_L2 + 18), i.plus(A_L2 + 9)
                prep(c)
                if side:
                    idx_add(i.plus(-1))
                evac(c.plus(1), a, qraw[:, i.mod(2), :])
                prep(c.plus(1))

            lagged(dve, tile_qi)

            def conv(n, k, c, a, dst):
                st = Steps(dve, s.conv_dve, 5, n)
                acc_wait(c.plus(1))
                TT(cbuf[:, 3:3 + T], acc[a.mod(2)][:, 0:T], rB, MUL).then_inc(s.evacuated, 1)
                dve.wait_ge(s.evacuated, a.value(1))
                st.step(TS(wk[:, 3, :], cbuf[:, 3:3 + T], convh[:, ds(k.value(36), 1)], convh[:, ds(k.value(48), 1)], MUL, ADD))
                for j in range(3):
                    st.wait()
                    st.step(STT(wk[:, 3, :], cbuf[:, j:j + T], convh[:, ds(k.value(12 * j), 1)], wk[:, 3, :], MUL, ADD))
                prep(c.plus(1))
                dve.wait_ge(s.conv_act, n.value(1))
                st.step(STT(dst, wk[:, 4, :], 1.0, wk[:, 3, :], ADD, MUL))

            def top(r):
                for h, w in ((0, score[:, 0:128]), (1, score[:, 128:384])):
                    dve.wait_ge(s.topk, r.times(4).value(2 * h + 1))
                    apart(dve)
                    V.max(mx8[:, 8 * h:8 * h + 8], w).then_inc(s.topk, 1)
                    dve.wait_ge(s.topk, r.times(4).value(2 * h + 2))
                    apart(dve)
                    V.match_replace(w, mx8[:, 8 * h:8 * h + 8], w, TAKEN).then_inc(s.topk, 1)
                dve.wait_ge(s.topk, r.times(4).value(5))

            for n in range(4):
                c, a = At(B_L2 + 34 + 2 * n), At(A_L2 + 17 + n)
                prep(c)
                if n == 0:
                    idx_add(At(7))
                    dve.wait_ge(s.causal_landed, 16)
                    TT(score, score, causal, ADD).then_inc(s.topk, 1)
                conv(At(n), At(8 + n), c, a, bc[:, n, :])

            def tile_xs(i, side):
                c, a = i.times(2).plus(B_L2 + 42), i.plus(A_L2 + 21)
                prep(c)
                top(i)
                conv(i.plus(4), i, c, a, tile(xs, i))

            lagged(dve, tile_xs)
            TS(score, score, 0.5 * TAKEN, NEG, ALU.is_gt, MUL).then_inc(s.topk, 1)
            dve.wait_ge(s.topk, 34)
            TT(score, score, causal, MIN).then_inc(s.topk, 1)
            dve.wait_ge(s.topk, 35)

            def side2(j, t):
                n, g = t.plus(8), t.mod(2)
                m = t.div(2).plus(4 * g)
                st = Steps(dve, s.ssd_dve, 3, t)
                if j == 0:
                    dve.wait_ge(s.ssd_bc, t.value(1))
                    TT(wk[:, 0:2, :].rearrange("p k (c l) -> p (k c) l", c=2), pG.rearrange("p (k l) -> p k l", k=4),
                       tril.unsqueeze(1).to_broadcast([P, 4, 128]), ADD).then_inc(s.ssd_em, 1)
                    attn_logits(n, score[:, 0:128], score[:, 128:384])
                if j == 1:
                    attn_norm(n)
                if j == 2:
                    dve.wait_ge(s.ssd_w, t.value(1))
                    for h in range(2):
                        w = W[:, 384 * h:384 * h + 384]
                        col = t.div(2).times(2).plus(8 * g + h)
                        STT(w[:, 0:256], w[:, 0:256], dt_tok[:, 0, ds(col.value(), 1)], cbt[:, g, 0:256], MUL, MUL)
                        last = STT(w[:, 256:384], w[:, 256:384], dt_tok[:, 1, ds(col.value(), 1)], cbt[:, g, 256:384], MUL, MUL)
                    last.then_inc(s.ssd_m, 1)
                if j == 3:
                    dve.wait_ge(s.ssd_y, t.value(1))
                    st.step(STT(wk[:, 6, :], tile(xs, m), pcol("d_skip", m), pV[:, 0:T], MUL, ADD))
                    dve.wait_ge(s.ssd_z, t.value(1))
                    st.step(STT(wk[:, 5, :], wk[:, 5, :], 1.0, zraw[:, g, :], ADD, MUL))
                    st.wait()
                    st.step(STT(tile(yz, m), wk[:, 6, :], 0.5, wk[:, 5, :], MUL, MUL))
                    attn_lo(n, tile(b_lo, n), tile(b_hi, n))

            W = wk[:, 2:5, :].rearrange("p k t -> p (k t)")

            def tile_qz(i, side):
                c, a = i.times(4).plus(B_L2 + 58), i.times(2).plus(A_L2 + 29)
                for j in range(4):
                    prep(c.plus(j))
                    if side and j < 3:
                        side2(j, i.plus(-1))
                    if j == 1:
                        evac(c.plus(1), a, qraw[:, i.mod(2), :])
                    if j == 3:
                        evac(c.plus(3), a.plus(1), zraw[:, i.mod(2), :])
                        head_norm(i.plus(5), qraw[:, i.mod(2), :], "g_q", qN[:, i.mod(2), :])
                        if side:
                            side2(3, i.plus(-1))

            lagged(dve, tile_qz)
            for j in range(4):
                side2(j, At(7))
            for g in range(2):
                rsqrt(At(17 + g), 1.0 / 512, (t1, t2)[g])
            clear_sums(4)
            for m in range(8):
                STT(yz[:, m, :], yz[:, m, :], pcol("g_ssd", m), (t1, t2)[m // 4], MUL, MUL).then_inc(s.gn_dve, 1)
                dve.wait_ge(s.gn_dve, m + 1)
                if m:
                    dve.wait_ge(s.gn_hi, m)
                    TT(b_lo[:, m - 1, :], yz[:, m - 1, :], b_hi[:, m - 1, :].bitcast(F32), SUB).then_inc(s.gn_ready, 1)
            dve.wait_ge(s.gn_hi, 8)
            TT(b_lo[:, 7, :], yz[:, 7, :], b_hi[:, 7, :].bitcast(F32), SUB).then_inc(s.gn_ready, 1)
            out_tiles(B_OUT2, A_OUT2, 3, "g_mlp2")
            mlp(B_MLP2, A_MLP2, 1, 19)

        @block.tensor
        def _(pe):
            MM = nc.tensor.matmul

            def chunk(c, a, hi, lo, k0, start=True, stop=True, cols=P):
                slot, ps = c.mod(NSLOT), acc[a.mod(2)]
                pe.wait_ge(s.lo_done, c.value(1))
                if start and a.least() >= 2:
                    pe.wait_ge(s.evacuated, a.value(-1))
                for k in range(KC):
                    wh, wl = (w[:, slot, P * k:P * k + P] for w in (whi, wlo))
                    MM(ps[:, 0:T], wh, hi[:, k0 + k, :], start=start and k == 0, stop=False)
                    MM(ps[:, 0:T], wh, lo[:, k0 + k, :], start=False, stop=False)
                    last = MM(ps[:, 0:T], wl, hi[:, k0 + k, :], start=False, stop=stop and k == KC - 1)
                last.then_inc(s.mm_done, 1)

            def stat(n, src, rows=P, dst=None):
                if n.least() > 0:
                    pe.wait_ge(s.var_ready, n.value())
                MM(pN[:, 0:T] if dst is None else dst, ones[0:rows, :], src, start=True, stop=True).then_inc(s.stat_ready, 1)

            def transposes(dst, srcs):
                for k, src in enumerate(srcs):
                    last = nc.tensor.transpose(dst[:, P * k:P * k + P], src, ident)
                return last

            def attn_scores(n, q, k):
                if n.least() > 0:
                    pe.wait_ge(s.logits_ready, n.value())
                MM(pS[:, 0:128], q[:, 0:128], k[:, 0:128], start=True, stop=True)
                MM(pS[:, 128:384], q[:, 128:256], k, start=True, stop=True).then_inc(s.scores_ready, 1)

            def attn_transpose(n):
                pe.wait_ge(s.probs_ready, n.value(1))
                if n.least() > 0:
                    pe.wait_ge(s.pt_copied, n.value())
                transposes(pT, [L[:, 128 * k:128 * k + 128] for k in range(3)]).then_inc(s.probs_transposed, 1)

            def attn_pv(n, v):
                pe.wait_ge(s.pt_copied, n.value(1))
                if n.least() > 0:
                    pe.wait_ge(s.attn_ready, n.value())
                MM(pO[:, 0:T], v[:, 0:128], PTs[:, 0:T], start=True, stop=False)
                MM(pO[:, 128:T], v[:, 128:256], PTs[:, T:384], start=False, stop=True).then_inc(s.pv_done, 1)

            def side1(j, t, p):
                b = l1[p]
                if j == 0:
                    pe.wait_ge(s.evacuated, t.times(8).value(8))
                    attn_scores(t, b.q, b.k)
                    if t.least() > 0:
                        pe.wait_ge(s.v_copied, t.value())
                    transposes(pV, [b.v[:, 0:128], b.v[:, 128:256]]).then_inc(s.v_transposed, 1)
                if j == 1:
                    pe.wait_ge(s.lru_dve, t.times(15).value(4))
                    pe.wait_ge(wg_landed[p], t.div(2).times(16).value(16))
                    w = wg[:, p, :]
                    MM(pG[:, 0:T], w[:, 0:128], wk[:, 0, :], start=True, stop=True)
                    MM(pG[:, T:2 * T], w[:, 128:256], wk[:, 0, :], start=True, stop=True).then_inc(s.lru_pe, 1)
                if j == 2:
                    attn_transpose(t)
                if j == 3:
                    pe.wait_ge(s.v_copied, t.value(1))
                    attn_pv(t, vtok)

            def bias_rows(j):
                for h in (2 * j, 2 * j + 1):
                    if h >= 2:
                        pe.wait_ge(s.bias_copied, h - 1)
                    MM((pG if h % 2 else pO)[:, 0:512], tab[0:33, h:h + 1].to_broadcast([33, P]), oh[0:33, :],
                       start=True, stop=True).then_inc(s.bias_ps, 1)

            def tile1(i, side):
                for j in range(8):
                    c, a = i.times(16).plus(2 * j), i.times(8).plus(j)
                    first = i.base == 0 and j == 0
                    if first:
                        pe.wait_ge(s.a_ready, 8)
                    chunk(c, a, a_hi, a_lo, 0, stop=False)
                    if first:
                        pe.wait_ge(s.a_ready, 16)
                    chunk(c.plus(1), a, a_hi, a_lo, 8, start=False)
                    if first:
                        pe.wait_ge(s.cst_landed, 16)
                        pe.wait_ge(s.sq_added, 16)
                        stat(At(0), sqacc[:, 0, :])
                        pe.wait_ge(s.oh_landed, 16)
                        pe.wait_ge(s.tab_landed, 16)
                    if i.base == 0 and j < 4:
                        bias_rows(j)
                    if i.base == 0 and j == 7:
                        pe.wait_ge(s.bias_copied, 8)
                    if side:
                        side1(j, i.plus(-1), (i.base + 1) % 2)

            lagged(pe, tile1)

            def mix(q, side):
                for h in range(2):
                    c = q.times(36).plus(B_Y + 18 * h)
                    a = q.times(24).plus(A_Y + 12 * h)
                    for j in range(6):
                        chunk(c.plus(2 * j), a.plus(j), a_hi, a_lo, 0, stop=False)
                        chunk(c.plus(2 * j + 1), a.plus(j), a_hi, a_lo, 8, start=False)
                        if side and h == 0:
                            side1(j, At(7), 1)
                    for k in range(2):
                        for n, g in enumerate((0, 2, 1)):
                            if side and h == 0 and k == 0:
                                pe.wait_ge((s.attn_ready, s.sc_dve, s.lru_dve)[n], (8, 40, 120)[n])
                            chunk(c.plus(12 + 3 * k + n), a.plus(6 + 3 * k + n), br[:, g, 0], br[:, g, 1], 0)

            mix(At(0), True)
            with pe.Fori(1, 4) as q:
                mix(At(0, (q, 1)), False)

            def unit(c, a, hi, lo, ready=None, n=0):
                if ready is not None:
                    pe.wait_ge(ready, n + 8)
                chunk(c, a, hi, lo, 0, stop=False)
                if ready is not None:
                    pe.wait_ge(ready, n + 16)
                chunk(c.plus(1), a, hi, lo, 8, start=False)

            pe.wait_ge(s.mix_ready, 8)
            with pe.Fori(0, 8) as i:
                for k in range(2):
                    unit(At(B_OUT1 + 2 * k, (i, 4)), At(A_OUT1 + k, (i, 2)), b_hi, b_lo, s.mix_ready, 0)

            def mlp(b, a, layer, norm, stage):
                for g in range(FF_GROUPS):
                    def up(m):
                        unit(m.times(2).plus(b + 64 * g), m.plus(a + 32 * g), a_hi, a_lo,
                             s.a_ready if g == 0 else None, 16 * stage)
                        if g == 0 and m.base == 0 and not m.terms:
                            pe.wait_ge(s.sq_added, 16 * stage + 16)
                            stat(At(norm), sqacc[:, 0, :])

                    def down(m):
                        unit(m.times(2).plus(b + 64 * g + 32), m.plus(a + 32 * g + 16), b_hi, b_lo,
                             s.hid_ready, 64 * layer + 16 * g)
                    up(At(0))
                    up(At(1))
                    with pe.Fori(1, 8) as j:
                        up(At(0, (j, 2)))
                        up(At(1, (j, 2)))
                    with pe.Fori(0, 7) as j:
                        down(At(0, (j, 2)))
                        down(At(1, (j, 2)))
                    down(At(14))
                    down(At(15))

            mlp(B_MLP1, A_MLP1, 0, 1, 1)

            unit(At(B_L2), At(A_L2), a_hi, a_lo, s.a_ready, 32)
            pe.wait_ge(s.sq_added, 48)
            stat(At(2), sqacc[:, 0, :])
            MM(pN[:, T:2 * T], ones, sqacc[:, 1, :], start=True, stop=True).then_inc(s.stat_ready, 1)

            def head_stat(n, rows=P):
                pe.wait_ge(s.nh_sq, n.value(1))
                stat(n.plus(4), sq[0:rows, 0, :], rows)

            for k in range(4):
                unit(At(B_L2 + 2 + 2 * k), At(A_L2 + 1 + k), a_hi, a_lo)
                if k == 0:
                    pe.wait_ge(s.sp_dve, 17)
                    transposes(pV, [sm_t[:, 0:128], sm_t[:, 128:256]]).then_inc(s.sm_pe, 1)
                head_stat(At(k), 64 if k == 0 else P)
                if k == 2:
                    pe.wait_ge(s.sm_dve, 3)
                    transposes(pT, [dtA[:, h // 2, 128 * (h % 2):128 * (h % 2) + 128] for h in range(4)])
                    MM(pS[:, 0:16], dtA[:, 1, 127:128].to_broadcast([P, P]), ident[:, R], start=True, stop=True)\
                        .then_inc(s.sm_pe, 1)
            for k in range(4):
                unit(At(B_L2 + 10 + 2 * k), At(A_L2 + 5 + k), a_hi, a_lo)
                if k == 0:
                    head_stat(At(4))
                    pe.wait_ge(s.sm_act, 1)
                else:
                    pe.wait_ge(s.vt_act, k)
                pe.wait_ge(s.evacuated, A_L2 + 6 + k)
                transposes(pV, [qraw[:, (1 + k) % 2, 128 * h:128 * h + 128] for h in range(2)]).then_inc(s.vt_pe, 1)

            def idx(n):
                pe.wait_ge(s.evacuated, n.value(A_L2 + 10))
                if n.least() > 0:
                    pe.wait_ge(s.idx_relu, n.value())
                q = qraw[:, n.mod(2), :]
                MM(pT[:, 0:T].rearrange("p (h k) -> p h k", h=2), q[:, 0:128],
                   kibd.rearrange("p (h k) -> p h k", h=2)[:, :, 0:128], start=True, stop=True)
                MM(pS[:, 0:2 * T], q[:, 128:256], kibd, start=True, stop=True).then_inc(s.idx_pe, 1)

            def tile_qi(i, side):
                unit(i.times(2).plus(B_L2 + 18), i.plus(A_L2 + 9), a_hi, a_lo)
                if side:
                    idx(i.plus(-1))
                else:
                    pe.wait_ge(s.sm_dma, 16)
                    pe.wait_ge(s.sm_act, 2)
                    pe.wait_ge(s.sm_dve, 4)

            lagged(pe, tile_qi)
            for n in range(4):
                unit(At(B_L2 + 34 + 2 * n), At(A_L2 + 17 + n), a_hi, a_lo)
                if n == 0:
                    idx(At(7))

            def xs_transpose(n):
                pe.wait_ge(s.xs_staged, n.value(1))
                if n.least() > 0:
                    pe.wait_ge(s.xt_act, n.value())
                transposes(pV, [xs_st[:, 0:128], xs_st[:, 128:256]]).then_inc(s.xt_pe, 1)

            def tile_xs(i, side):
                unit(i.times(2).plus(B_L2 + 42), i.plus(A_L2 + 21), a_hi, a_lo)
                if side:
                    xs_transpose(i.plus(-1))
                else:
                    pe.wait_ge(s.conv_dve, 20)
                    pe.wait_ge(s.vt_act, 4)
                    for g, ps in ((0, pG), (1, pO)):
                        MM(ps[:, 0:T], bc[:, g, 0:128], bc[:, 2 + g, :], start=True, stop=True)
                        last = MM(ps[:, T:384], bc[:, g, 128:256], bc[:, 2 + g, 128:256], start=True, stop=True)
                    last.then_inc(s.cb_pe, 1)

            lagged(pe, tile_xs)

            def side2(j, t):
                n, g = t.plus(8), t.mod(2)
                if j == 0:
                    pe.wait_ge(s.staged, t.value(1))
                    if t.least() > 0:
                        pe.wait_ge(s.ssd_w, t.value())
                    for h in range(2):
                        last = MM(pG[:, T * h:T * h + T], col_st[:, h:h + 1].to_broadcast([P, P]), dtA[:, 1, :],
                                  start=True, stop=True)
                    last.then_inc(s.ssd_bc, 1)
                    pe.wait_ge(s.nh_ready, t.value(6))
                    attn_scores(n, qN[:, t.mod(2), :], tile(kN, t.div(2)))
                if j == 2:
                    attn_transpose(n)
                if j == 3:
                    pe.wait_ge(s.ssd_m, t.value(1))
                    if t.least() > 0:
                        pe.wait_ge(s.ssd_dve, t.times(3).value(-2))
                    W = wk[:, 2:5, :].rearrange("p k t -> p (k t)")
                    for h in range(2):
                        y = pV[64 * h:64 * h + 64]
                        MM(y[:, 0:T], xt_st[:, 64 * h:64 * h + 64], W[:, 384 * h:384 * h + 256], start=True, stop=False)
                        last = MM(y[:, 128:T], xt_st[:, 128 + 64 * h:128 + 64 * h + 64], W[:, 384 * h + 256:384 * h + 384], start=False, stop=True)
                    last.then_inc(s.ssd_y, 1)
                    attn_pv(n, v_st)

            def tile_qz(i, side):
                c, a = i.times(4).plus(B_L2 + 58), i.times(2).plus(A_L2 + 29)
                for j in range(4):
                    chunk(c.plus(j), a.plus(j // 2), a_hi, a_lo, 8 * (j % 2), start=j % 2 == 0, stop=j % 2 == 1)
                    if side:
                        side2(j, i.plus(-1))
                    elif j == 0:
                        pe.wait_ge(s.conv_dve, 60)
                        xs_transpose(At(7))
                        pe.wait_ge(s.cb_act, 1)
                    if j == 3:
                        head_stat(i.plus(5))

            lagged(pe, tile_qz)
            for j in range(4):
                side2(j, At(7))
            for g in range(2):
                pe.wait_ge(s.ssd_sum, 7 + g)
                stat(At(17 + g), sqacc[:, g, :])
            with pe.Fori(0, 8) as i:
                for k in range(2):
                    c, a = At(B_OUT2 + 2 * k, (i, 4)), At(A_OUT2 + k, (i, 2))
                    pe.wait_ge(s.attn_ready, 16)
                    chunk(c, a, b_hi, b_lo, 8, stop=False)
                    pe.wait_ge(s.gn_ready, 8)
                    chunk(c.plus(1), a, b_hi, b_lo, 0, start=False)
            mlp(B_MLP2, A_MLP2, 1, 19, 3)


def blocks(w):
    k, n = w.shape
    return w.reshape(k // (KC * P), KC, P, n // P, P).transpose(3, 0, 2, 1, 4).reshape(n // P, k // (KC * P), P, CW)


def columns(v):
    return v.reshape(-1, P).T


def distance_rows():
    oh = np.zeros((33, 512), np.float32)
    for c in range(512):
        dist = 256 - c
        if dist < 0 or dist > 255:
            oh[32, c] = NEG
        elif dist < 16:
            oh[dist, c] = 1.0
        else:
            oh[min(31, 16 + int(np.log(np.float32(dist) / 16) / np.log(8.0) * 16 + 1e-9)), c] = 1.0
    return oh


def kernel(**inputs):
    import concourse.bacc as bacc
    from concourse.bass_utils import run_bass_kernel_spmd

    a = {n: np.asarray(v) for n, v in inputs.items()}
    w1, w2 = a["w_in"][0], a["w_in_2"][0]
    b1 = blocks(w1)
    parts = [b1[[8 * k + i for k in (0, 1, 2, 3, 4, 6, 7, 5)]] for i in range(8)]
    ya, yb, yc = (blocks(a[n][0]) for n in ("w_attn_o", "w_lru_o", "w_sc_o"))
    for m in range(0, 16, 2):
        parts += [b1[[64 + 16 * k + m + j for j in range(2) for k in range(3)]]]
        parts += [y[m + j] for j in range(2) for y in (ya, yc, yb)]
    parts += [blocks(a["w_out"][0])]

    def mlp(up, down):
        u, d = blocks(up), blocks(down)
        for g in range(FF_GROUPS):
            yield u[16 * g:16 * g + 16]
            yield d[:, 2 * g:2 * g + 2]

    parts += mlp(a["w_mlp_up"][0], a["w_mlp_down"][0])
    small = np.concatenate([w2[:, 5648:5728], w2[:, 2544:2576]], 1)
    small = np.concatenate([small, np.zeros((D, P - small.shape[1]), np.float32)], 1)
    cols = lambda lo, hi: blocks(np.ascontiguousarray(w2[:, lo:hi]))
    z, q = cols(0, 1024), cols(2576, 3600)
    parts += [blocks(small), cols(3600, 4112), cols(4112, 4624), cols(4624, 5648), cols(2048, 2560), cols(1024, 2048)]
    for r in range(8):
        parts += [q[r:r + 1], z[r // 2 + 4 * (r % 2)][None]]
    parts += [blocks(a["w_out_2"][0])[:, ::-1]]
    parts += mlp(a["w_up_2"][0], a["w_down_2"][0])
    stream = np.concatenate([p.reshape(-1, P, CW) for p in parts])
    assert stream.shape[0] == CHUNKS

    par = np.zeros((P, N_PARAMS), np.float32)

    def put(name, v):
        par[:v.shape[0], PARAMS[name]:PARAMS[name] + v.shape[1]] = v

    for name, key in (("g_mix1", "norm_mix_g"), ("gate_b", "gate_b"), ("lru_w", "lru_conv_w"), ("lru_b", "lru_conv_b"),
                      ("lru_ba", "lru_ba"), ("lru_bx", "lru_bx"), ("lam", "lru_lambda"), ("sc_w", "sc_conv_w"),
                      ("g_mlp1", "norm_mlp_g"), ("final_g", "final_g"), ("g_mix2", "g_mix_2"), ("conv_w", "conv_w_2"),
                      ("conv_b", "conv_b_2"), ("g_mlp2", "g_mlp_2"), ("g_ssd", "g_ssd_2"), ("g_q", "g_q_2"), ("g_k", "g_k_2")):
        put(name, columns(a[key]))
    put("d_skip", columns(np.repeat(a["d_skip_2"][0], 64)))
    put("g_kidx", a["g_kidx_2"].T)
    par[DT_ROW:DT_ROW + 16, PARAMS["dt_bias"]] = a["dt_bias_2"][0]
    par[DT_ROW:DT_ROW + 16, PARAMS["a_log"]] = a["a_log_2"][0]

    i = np.arange(P)
    late = np.where(i[None, :] > i[:, None], NEG, 0.0)
    consts = np.concatenate([np.eye(P), np.ones((P, P)), late.T, late, np.zeros((P, P)), late], 1).astype(np.float32)
    arrays = {
        "x": a["x"][0].T.reshape(DT, P, T).transpose(1, 0, 2),
        "stream": stream,
        "gates": np.stack([a["lru_wa"][0], a["lru_wx"][0]], 2).transpose(1, 0, 2, 3).reshape(P, 8 * T),
        "params": par,
        "consts": consts,
        "onehot": distance_rows(),
        "table": np.concatenate([a["rel_table"], np.ones((1, HEADS), np.float32)]),
    }
    arrays = {n: np.ascontiguousarray(v) for n, v in arrays.items()}
    nc = bacc.Bacc("TRN2", target_bir_lowering=False, num_devices=1)
    aps = [nc.dram_tensor(n, v.shape, F32, kind="ExternalInput").ap() for n, v in arrays.items()]
    by = dict(zip(arrays, aps))
    scratch = nc.dram_tensor("bias_scratch", (HEADS, P * 512), F32, kind="Internal").ap()
    out = nc.dram_tensor("out", (P, DT, T), F32, kind="ExternalOutput").ap()
    program(nc, by["x"], by["stream"], by["gates"], by["params"], by["consts"], by["onehot"], by["table"], scratch, out)
    r = run_bass_kernel_spmd(nc, [arrays], core_ids=[0])
    got = r.results[0]["out"]
    return np.ascontiguousarray(got.transpose(1, 0, 2).reshape(D, T).T)[None]
```
